# Optimizing a Trainium2 kernel written in Bass

```python
import jax, jax.numpy as jnp
from jax import lax
import numpy as np

D_MODEL = 1024
BATCH = 1
SEQ = 1024
DEPTH = 1

CHUNK = 64
Q_BLOCK = 128
SB_HEAD_DIM = 64
SB_WIDTH = D_MODEL // 2
SB_HEADS = SB_WIDTH // SB_HEAD_DIM
GLA_HEADS = 4
GLA_K_WIDTH = D_MODEL // 4
GLA_V_WIDTH = D_MODEL // 2
GLA_KEY_DIM = GLA_K_WIDTH // GLA_HEADS
GLA_VAL_DIM = GLA_V_WIDTH // GLA_HEADS
GLA_RANK = 16
GLA_GATE_TEMP = 16.0
N_BRANCH = 2
EPS = 1e-6

IN_SPLITS = (SB_WIDTH, SB_WIDTH, SB_WIDTH, SB_WIDTH,
             GLA_K_WIDTH, GLA_K_WIDTH, GLA_V_WIDTH, GLA_V_WIDTH,
             GLA_RANK,
             D_MODEL, D_MODEL)
N_IN = 4 * SB_WIDTH + 2 * GLA_K_WIDTH + 2 * GLA_V_WIDTH + GLA_RANK + N_BRANCH * D_MODEL

kernel_name = "stickbreak_gla_gated_hybrid"

def _rmsnorm(x, g):
    xf = x.astype(jnp.float32)
    y = xf * lax.rsqrt(jnp.mean(xf * xf, axis=-1, keepdims=True) + EPS)
    return y.astype(x.dtype) * g

def _heads(t, n_heads):
    b, s, w = t.shape
    return t.reshape(b, s, n_heads, w // n_heads).transpose(0, 2, 1, 3)

def _merge_heads(t):
    b, h, s, d = t.shape
    return t.transpose(0, 2, 1, 3).reshape(b, s, h * d)

def _stick_breaking(q, k, v):
    seq = q.shape[2]
    scale = q.shape[-1] ** -0.5
    outs = []
    for blk in range(seq // Q_BLOCK):
        start = blk * Q_BLOCK
        end = start + Q_BLOCK
        qb = q[:, :, start:end]
        kb = k[:, :, :end]
        vb = v[:, :, :end]
        z = jnp.einsum('bhqd,bhkd->bhqk', qb, kb).astype(jnp.float32) * scale
        t_idx = start + jnp.arange(Q_BLOCK)[:, None]
        s_idx = jnp.arange(end)[None, :]
        mask = s_idx < t_idx
        log_one_minus = jnp.where(mask, jax.nn.log_sigmoid(-z), 0.0)
        suffix = lax.cumsum(log_one_minus, axis=3, reverse=True) - log_one_minus
        weights = jnp.where(mask, jnp.exp(jax.nn.log_sigmoid(z) + suffix), 0.0)
        outs.append(jnp.einsum('bhqk,bhkd->bhqd', weights.astype(vb.dtype), vb))
    return jnp.concatenate(outs, axis=2)

def _gla_chunked(q, k, v, log_alpha):
    b_, h_, s_, dk = q.shape
    dv = v.shape[-1]
    n = s_ // CHUNK
    scale = dk ** -0.5
    q = q.reshape(b_, h_, n, CHUNK, dk)
    k = k.reshape(b_, h_, n, CHUNK, dk)
    v = v.reshape(b_, h_, n, CHUNK, dv)
    cum = lax.cumsum(log_alpha.reshape(b_, h_, n, CHUNK, dk), axis=3)
    cum_last = cum[:, :, :, -1:, :]
    q_dec = q * jnp.exp(cum) * scale
    k_inv = k * jnp.exp(-cum)
    k_to_end = k * jnp.exp(cum_last - cum)
    causal = jnp.tril(jnp.ones((CHUNK, CHUNK), dtype=bool))
    scores = jnp.where(causal, jnp.einsum('bhnqd,bhnsd->bhnqs', q_dec, k_inv), 0.0)
    o_intra = jnp.einsum('bhnqs,bhnsv->bhnqv', scores, v)
    kv_chunk = jnp.einsum('bhnsd,bhnsv->bhndv', k_to_end, v)
    chunk_decay = jnp.exp(cum_last[:, :, :, 0, :])

    def step(state, inp):
        dec, kv = inp
        return dec[..., None] * state + kv, state

    init = jnp.zeros((b_, h_, dk, dv), kv_chunk.dtype)
    _, s_prev = lax.scan(step, init, (jnp.moveaxis(chunk_decay, 2, 0), jnp.moveaxis(kv_chunk, 2, 0)))
    s_prev = jnp.moveaxis(s_prev, 0, 2)
    o_inter = jnp.einsum('bhnqd,bhndv->bhnqv', q_dec, s_prev)
    return (o_intra + o_inter).reshape(b_, h_, s_, dv)

def setup_inputs(seed: int = 0) -> dict:
    key = jax.random.key(seed)
    ks = jax.random.split(key, 12)
    f32 = jnp.float32
    x = jax.random.normal(ks[0], (BATCH, SEQ, D_MODEL), f32)
    g_pre = 1.0 + 0.02 * jax.random.normal(ks[1], (DEPTH, D_MODEL), f32)
    w_in = jax.random.normal(ks[2], (DEPTH, D_MODEL, N_IN), f32) * D_MODEL ** -0.5
    b_gate = 0.01 * jax.random.normal(ks[3], (DEPTH, N_BRANCH * D_MODEL), f32)
    w_alpha_up = jax.random.normal(ks[4], (DEPTH, GLA_RANK, GLA_K_WIDTH), f32) * GLA_RANK ** -0.5
    b_alpha_up = 0.01 * jax.random.normal(ks[5], (DEPTH, GLA_K_WIDTH), f32)
    g_gla_norm = 1.0 + 0.02 * jax.random.normal(ks[6], (DEPTH, GLA_VAL_DIM), f32)
    w_o_sb = jax.random.normal(ks[7], (DEPTH, SB_WIDTH, D_MODEL), f32) * SB_WIDTH ** -0.5
    w_o_gla = jax.random.normal(ks[8], (DEPTH, GLA_V_WIDTH, D_MODEL), f32) * GLA_V_WIDTH ** -0.5
    w_out = jax.random.normal(ks[9], (DEPTH, D_MODEL, D_MODEL), f32) * D_MODEL ** -0.5
    g_final = 1.0 + 0.02 * jax.random.normal(ks[10], (D_MODEL,), f32)
    return {"x": x, "g_pre": g_pre, "w_in": w_in, "b_gate": b_gate,
            "w_alpha_up": w_alpha_up, "b_alpha_up": b_alpha_up, "g_gla_norm": g_gla_norm,
            "w_o_sb": w_o_sb, "w_o_gla": w_o_gla, "w_out": w_out, "g_final": g_final}

def reference(x, g_pre, w_in, b_gate, w_alpha_up, b_alpha_up, g_gla_norm,
              w_o_sb, w_o_gla, w_out, g_final):
    split_at = [int(c) for c in np.cumsum(IN_SPLITS)[:-1]]
    for layer in range(DEPTH):
        h = _rmsnorm(x, g_pre[layer])
        proj = jnp.einsum('bsd,dn->bsn', h, w_in[layer])
        (sb_q, sb_k, sb_v, sb_z, gla_q, gla_k, gla_v, gla_z,
         gla_lr, gate_logits) = jnp.split(proj, split_at, axis=-1)[:10] + [None] if False else \
            tuple(jnp.split(proj[..., :split_at[-2]], split_at[:-2], axis=-1)) + (proj[..., split_at[-2]:],)

        o_sb = _merge_heads(_stick_breaking(_heads(sb_q, SB_HEADS), _heads(sb_k, SB_HEADS),
                                            _heads(sb_v, SB_HEADS)))
        y_sb = jnp.einsum('bsw,wd->bsd', (o_sb * jax.nn.silu(sb_z)).astype(x.dtype), w_o_sb[layer])

        alpha_logit = jnp.einsum('bsr,rk->bsk', gla_lr, w_alpha_up[layer]) + b_alpha_up[layer]
        log_alpha = jax.nn.log_sigmoid(alpha_logit.astype(jnp.float32)) / GLA_GATE_TEMP
        o_gla = _gla_chunked(_heads(gla_q, GLA_HEADS), _heads(gla_k, GLA_HEADS),
                             _heads(gla_v, GLA_HEADS), _heads(log_alpha, GLA_HEADS))
        o_gla = _merge_heads(_rmsnorm(o_gla, g_gla_norm[layer]))
        y_gla = jnp.einsum('bsw,wd->bsd', (o_gla * jax.nn.silu(gla_z)).astype(x.dtype), w_o_gla[layer])

        gates = jax.nn.sigmoid(gate_logits + b_gate[layer])
        g_sb, g_gla = gates[..., :D_MODEL], gates[..., D_MODEL:]
        merged = g_sb * y_sb + g_gla * y_gla
        x = x + jnp.einsum('bsd,de->bse', merged, w_out[layer])
    return _rmsnorm(x, g_final)


_drawn_inputs = setup_inputs


def setup_inputs(seed=0):
    import zlib

    import numpy as np

    out = dict(_drawn_inputs(seed))
    spreads = {}
    factors = {'g_pre': 3.721,
     'b_gate': 28.864,
     'b_alpha_up': 24.25,
     'g_gla_norm': 23.582,
     'g_final': 8.487}
    for name, (base, spread) in spreads.items():
        noise = np.random.default_rng([zlib.crc32(name.encode()), seed]).standard_normal(out[name].shape)
        drawn = base * np.exp(spread * noise) if base else spread * noise
        out[name] = __import__('jax').numpy.asarray(drawn.astype(out[name].dtype))
    for name, factor in factors.items():
        out[name] = (out[name] * factor).astype(out[name].dtype)
    return out
```

```python
from contextlib import ExitStack

import concourse.bass as bass
from concourse import mybir

ALU = mybir.AluOpType
ACT = mybir.ActivationFunctionType
F32 = mybir.dt.float32
F32R = mybir.dt.float32r
BF16 = mybir.dt.bfloat16
I32 = mybir.dt.int32

P = 128
HALF = 512
NEG = -1.0e30
EPS = 1e-6

D = 1024
SEQ = 1024
SBW = D // 2
HD = 64
GKW = D // 4
GVW = D // 2
DV = 128
CH = 64
RANK = 16
KT = D // P
ST = SEQ // P
PAIRS = SBW // P
NCH = SEQ // CH

COL_Q, COL_K, COL_V, COL_Z = 0, SBW, 2 * SBW, 3 * SBW
COL_GQ = 4 * SBW
COL_GK = COL_GQ + GKW
COL_GV = COL_GK + GKW
COL_GZ = COL_GV + GVW
COL_LR = COL_GZ + GVW
COL_GA = COL_LR + RANK
COL_GB = COL_GA + D

MM_HALF = KT * 3
STEPS = 18
SHARE = [8, 9, 10, 11, 11, 12, 13, 14] * 2 + [8, 8]


def plan_projection(tiles):
    work = [(j, h, k, p) for j in range(tiles) for h in range(2) for k in range(KT) for p in range(3)]
    steps, at, total = [], 0, 0
    for share in SHARE:
        total += share
        to = len(work) * total // sum(SHARE)
        steps.append(work[at:to])
        at = to
    return steps


def plan_rounds():
    rounds = []
    for step in range(STEPS):
        if step in (1, 2):
            rounds.append(("v", step, step - 1))
        if 1 <= step <= 16:
            unit = step - 1
            blocks = unit % 8 + 1
            for b in range(0, blocks, 4):
                rounds.append(("w", step, unit, b, min(4, blocks - b)))
    return rounds


ROUNDS = plan_rounds()
RPP = len(ROUNDS)
R0 = 16
LAST_ROUND = {r[2]: n for n, r in enumerate(ROUNDS) if r[0] == "w"}


def stickbreak_gla_hybrid(nc, x, g_pre, w_in, b_gate, w_alpha_up, b_alpha_up, g_gla_norm,
                          w_o_sb, w_o_gla, w_out, g_final, out):
    x_rows = x[0].rearrange("(t p) d -> t p d", p=P)
    out_rows = out[0].rearrange("(t p) d -> t p d", p=P)
    w_in_v = w_in[0].rearrange("(k p) c -> p k c", p=P)
    wo_sb_v = w_o_sb[0].rearrange("(k p) c -> p k c", p=P)
    wo_gla_v = w_o_gla[0].rearrange("(k p) c -> p k c", p=P)
    w_out_v = w_out[0].rearrange("(k p) c -> p k c", p=P)

    with ExitStack() as ctx:
        base = (nc.sbuf_base + 63) // 64 * 64
        K = 1024

        def at(name, kb, shape, dt=F32):
            return nc.alloc_sbuf_tensor_at(name, shape, dt, offset=base + int(kb * K))

        w_raw = at("w_raw", 0, [P, 2, KT, P])
        w_hi = at("w_hi", 8, [P, 2, KT, P], F32R)
        w_lo = at("w_lo", 16, [P, 2, KT, P], F32R)
        ident = at("ident", 24, [P, P])
        ident_bf = at("ident_bf", 24.5, [P, P], BF16)
        mask_neg = at("mask_neg", 24.75, [P, P], BF16)
        vec_rows = at("vec_rows", 25, [27, P])
        cols = at("cols", 25.5, [P, 27])
        stats = at("stats", 25.75, [P, 64])
        w_lr = at("w_lr", 26, [P, KT, 2 * RANK], F32R)
        w_up = at("w_up", 27, [2 * RANK, GKW])
        h_hi = at("h_hi", 28, [P, KT, SEQ], F32R)
        h_lo = at("h_lo", 60, [P, KT, SEQ], F32R)
        G = at("G", 92, [P, 8, SEQ])
        F = 124
        x_t = at("x_t", F, [P, ST, D])
        junk = at("junk", F + 32, [P, D])
        lr_raw = at("lr_raw", F + 36, [P, KT, RANK])
        wt_hi = [at("wt_hi0", 108, [P, 6, 256], F32R), at("wt_hi1", F + 8, [P, 8, 256], F32R)]
        wt_lo = [at("wt_lo0", 114, [P, 6, 256], F32R), at("wt_lo1", F + 16, [P, 8, 256], F32R)]
        stage_q = at("stage_q", F, [P, SEQ])
        stage_k = at("stage_k", F + 4, [P, SEQ])
        q_st = [at(f"q_st{e}", F + 24 + 4 * e, [P, SEQ], F32R) for e in range(2)]
        k_hi = [at(f"k_hi{e}", F + 32 + 4 * e, [P, SEQ], F32R) for e in range(2)]
        k_lo = [at(f"k_lo{e}", F + 40 + 4 * e, [P, SEQ], F32R) for e in range(2)]
        v_t = at("v_t", F + 48, [P, SEQ])
        v_st = at("v_st", F + 52, [P, 2, ST, P], F32R)
        surv = at("surv", F + 60, [P, 2, SEQ + 8])
        beta = at("beta", F + 68.125, [P, 2, SEQ])
        z_silu = at("z_silu", F + 76.25, [P, SEQ])
        z_sig = at("z_sig", 120, [P, HALF])
        o_low = at("o_low", 122, [P, 2, 256])
        reset = at("reset", F + 8, [P, SEQ])
        t12 = at("t12", F + 12, [P, 2, SEQ])
        t3 = at("t3", F + 20, [P, SEQ])
        q_dec = at("q_dec", F + 24, [P, SEQ])
        k_inv = at("k_inv", F + 28, [P, SEQ])
        k_end = at("k_end", F + 32, [P, ST, P])
        v_nat = at("v_nat", F + 36, [P, ST, 2 * DV])
        state = at("state", F + 44, [P, NCH, DV])
        gv_t = at("gv_t", F + 52, [P, SEQ])
        sT = at("sT", F + 56, [P, 2, ST, P])
        gz = at("gz", F + 64, [P, 2, SEQ])
        gz_sig = at("gz_sig", F + 72, [P, HALF])
        mask4 = at("mask4", F + 74, [P, 4, P])
        lr_t = at("lr_t", F + 76, [2 * RANK, SEQ])
        o_nat = t12[:, :, :].rearrange("p a (b c) -> p a b c", b=ST)
        g_hi = at("g_hi", F, [P, 8, SEQ], F32R)
        g_lo = at("g_lo", F + 32, [P, 8, SEQ], F32R)
        gate = at("gate", F + 64, [P, 2, SEQ])
        gate_bias = at("gate_bias", F + 80, [P, 2, 2])
        y_g = at("y_g", F + 72, [P, 2, 2, HALF])
        mT = at("mT", 92, [P, KT, SEQ])
        wout_raw = at("wout_raw", 28, [P, KT, D])
        wout_hi = [at("wout_hi0", 60, [P, KT, HALF], F32R), at("wout_hi1", F, [P, KT, HALF], F32R)]
        wout_lo = [at("wout_lo0", 76, [P, KT, HALF], F32R), at("wout_lo1", F + 16, [P, KT, HALF], F32R)]
        x_res = at("x_res", F + 32, [P, 2, D])
        y_row = at("y_row", F + 40, [P, 2, D])
        y_out = at("y_out", F + 48, [P, 2, D])
        g_fin = at("g_fin", F + 56, [P, D])
        junk5 = at("junk5", F + 60, [P, D])
        g_fin_row = at("g_fin_row", F + 64, [1, D])

        def bank(name, n=1):
            return ctx.enter_context(nc.psum_tensor(name, [P, n * HALF], F32))

        pj = [bank("pj0"), bank("pj1")]
        tr = [bank("tr0"), bank("tr1")]
        sc = bank("sc", 2)
        ob = [bank("ob0"), bank("ob1")]
        ring4 = [sc[:, 0:HALF], sc[:, HALF:2 * HALF], ob[0][:, :], ob[1][:, :]]

        def sem(name):
            return ctx.enter_context(nc.semaphore(name))

        const_done = sem("const_done")
        vec_loaded = sem("vec_loaded")
        vec_turned = sem("vec_turned")
        cols_ready = sem("cols_ready")
        x_loaded = [sem(f"x_loaded{t}") for t in range(ST)]
        sq_done = sem("sq_done")
        rstd_ready = sem("rstd_ready")
        x_normed = sem("x_normed")
        lr_loaded = sem("lr_loaded")
        lr_split = sem("lr_split")
        raw_loaded = [sem("raw_loaded0"), sem("raw_loaded1")]
        hi_done = sem("hi_done")
        lo_done = sem("lo_done")
        proj_ready = sem("proj_ready")
        proj_act = sem("proj_act")
        proj_free = sem("proj_free")
        stack_hi = sem("stack_hi")
        stack_ready = sem("stack_ready")
        scores_ready = sem("scores_ready")
        sig_done = sem("sig_done")
        scan_done = sem("scan_done")
        w_ready = sem("w_ready")
        tr_ready = sem("tr_ready")
        tr_act = sem("tr_act")
        tr_free = sem("tr_free")
        av_done = sem("av_done")
        o_copied = sem("o_copied")
        o_free = sem("o_free")
        g_done = sem("g_done")
        q4_ready = sem("q4_ready")
        q4_act = sem("q4_act")
        q4_free = sem("q4_free")
        act_step = sem("act_step")
        dve_step = sem("dve_step")
        bias_ready = sem("bias_ready")
        slot_seen = sem("slot_seen")
        gate_ready = sem("gate_ready")
        gate_free = sem("gate_free")
        y_ready = sem("y_ready")
        y_free = sem("y_free")
        m_ready = sem("m_ready")
        gs_hi = sem("gs_hi")
        gs_lo = sem("gs_lo")
        wout_loaded = [sem(f"wout_loaded{c}") for c in range(4)]
        wout_h = sem("wout_h")
        wout_l = sem("wout_l")
        fin_loaded = sem("fin_loaded")
        fin_bc = sem("fin_bc")
        xr_loaded = [sem("xr_loaded0"), sem("xr_loaded1")]
        o5_ready = sem("o5_ready")
        o5_free = sem("o5_free")
        ss5 = sem("ss5")
        rstd5 = sem("rstd5")
        y_done = sem("y_done")
        stored = [sem("stored0"), sem("stored1")]

        block = ctx.enter_context(nc.Block())

        N3, N4, N5 = 18, 28, 28 + 3 * KT
        BODY = {0: [("v", 0), ("v", 1), ("z", 0), ("z", 1), ("q", 1), ("k", 1)],
                1: [("v", 2), ("v", 3), ("z", 2), ("z", 3)]}

        def bank_no(n):
            return 2 * n + (2 if n >= N3 else 0)

        def body_tile(hp, j):
            return N3 + (6 if hp else 0) + j

        def body_col(kind, n):
            return {"v": COL_GV, "z": COL_GZ, "q": COL_GQ, "k": COL_GK}[kind] + P * n

        R3 = R0 + RPP * PAIRS
        R_BODY = 10
        Q_BODY = 2 + (NCH - 1) + 4 + 4

        def load_small(sp):
            sp.dma_start(vec_rows[0:8, :], g_pre[0].rearrange("(a p) -> a p", p=P)).then_inc(vec_loaded, 16)
            sp.dma_start(vec_rows[8:24, :], b_gate[0].rearrange("(a p) -> a p", p=P)).then_inc(vec_loaded, 16)
            sp.dma_start(vec_rows[24:26, :], b_alpha_up[0].rearrange("(a p) -> a p", p=P))\
                .then_inc(vec_loaded, 16)
            sp.dma_start(vec_rows[26:27, :], g_gla_norm).then_inc(vec_loaded, 16)
            for c in range(2):
                sp.dma_start(w_up[RANK * c:RANK * (c + 1), :], w_alpha_up[0]).then_inc(vec_loaded, 16)

        @block.sync
        def _(sp):
            for t in range(ST):
                sp.dma_start(x_t[:, t, :], x_rows[t]).then_inc(x_loaded[t], 16)
                if t == 3:
                    load_small(sp)
            sp.dma_start(lr_raw[:, :, :], w_in_v[:, :, COL_LR:COL_LR + RANK]).then_inc(lr_loaded, 16)

            def load(n, col, slot):
                if not isinstance(n, int):
                    col = sp.snap(col)
                if not isinstance(n, int) or n >= 2:
                    sp.wait_ge(lo_done, n - 1)
                sp.dma_start(w_raw[:, slot, :, :], w_in_v[:, :, bass.ds(col, P)])\
                    .then_inc(raw_loaded[slot], 16)

            for n, col in enumerate((COL_Q, COL_K, COL_V)):
                load(n, col, n % 2)
            with sp.Fori(0, PAIRS - 1) as i:
                load(4 * i + 3, COL_Z + P * i, 1)
                load(4 * i + 4, COL_Q + P + P * i, 0)
                load(4 * i + 5, COL_K + P + P * i, 1)
                load(4 * i + 6, COL_V + P + P * i, 0)
            load(15, COL_Z + P * (PAIRS - 1), 1)
            load(16, COL_GQ, 0)
            load(17, COL_GK, 1)
            for hp in range(2):
                for j, (kind, m) in enumerate(BODY[hp]):
                    load(body_tile(hp, j), body_col(kind, m), body_tile(hp, j) % 2)
            with sp.Fori(0, KT // 2) as jj:
                for u in range(2):
                    n = 6 * jj + N4 + 3 * u
                    load(n, jj * (2 * P) + COL_GA + P * u, (N4 + 3 * u) % 2)
                    load(n + 1, jj * (2 * P) + COL_GB + P * u, (N4 + 3 * u + 1) % 2)
                    slot = (N4 + 3 * u + 2) % 2
                    c = jj * (2 * P) + P * u
                    sp.wait_ge(lo_done, n + 1)
                    sp.sem_inc(slot_seen, 1)
                    sp.dma_start(w_raw[:, slot, 0:4, :], wo_sb_v[:, :, bass.ds(c, P)])\
                        .then_inc(raw_loaded[slot], 16)
                    sp.dma_start(w_raw[:, slot, 4:8, :], wo_gla_v[:, :, bass.ds(c, P)])\
                        .then_inc(lr_loaded, 16)
            sp.wait_ge(gate_ready, 4 * KT)
            for c in range(4):
                e, kk = c // 2, 4 * (c % 2)
                sp.dma_start(wout_raw[:, kk:kk + 4, e * HALF:(e + 1) * HALF],
                             w_out_v[:, kk:kk + 4, e * HALF:(e + 1) * HALF]).then_inc(wout_loaded[c], 16)
            sp.wait_ge(m_ready, 2 * KT)
            sp.dma_start(g_fin_row[0:1, :], g_final.rearrange("(a d) -> a d", a=1)).then_inc(fin_loaded, 16)
            for t in range(ST):
                if t >= 2:
                    sp.wait_ge(o5_free, 2 * (t - 2) + 2)
                sp.dma_start(x_res[:, t % 2, :], x_rows[t]).then_inc(xr_loaded[t % 2], 16)
                if t >= 1:
                    sp.wait_ge(y_done, t)
                    sp.dma_start(out_rows[t - 1], y_out[:, (t - 1) % 2, :]).then_inc(stored[(t - 1) % 2], 16)
            sp.wait_ge(y_done, ST)
            sp.dma_start(out_rows[ST - 1], y_out[:, (ST - 1) % 2, :]).then_inc(stored[(ST - 1) % 2], 16)
            for s in stored:
                sp.wait_ge(s, 16 * ST // 2)

        @block.gpsimd
        def _(pool):
            pool.memset(ident[:, :], 0.0).then_inc(const_done, 1)
            pool.memset(ident_bf[:, :], 0.0).then_inc(const_done, 1)
            pool.memset(mask_neg[:, :], 0.0).then_inc(const_done, 1)
            pool.wait_ge(const_done, 3)
            for m in (ident, ident_bf):
                pool.affine_select(out=m[:, :], in_=m[:, :], compare_op=ALU.not_equal, fill=1.0, base=0,
                                   pattern=[[-1, P]], channel_multiplier=1).then_inc(const_done, 1)
            pool.affine_select(out=mask_neg[:, :], in_=mask_neg[:, :], compare_op=ALU.is_gt, fill=NEG,
                               base=0, pattern=[[-1, P]], channel_multiplier=1).then_inc(const_done, 1)
            pool.wait_ge(o_free, 2 + 8 * PAIRS)
            pool.memset(mask4[:, :, :], 1.0).then_inc(const_done, 1)
            pool.memset(reset[:, :], 1.0).then_inc(const_done, 1)
            pool.memset(sT[:, :, :, :], 0.0).then_inc(const_done, 1)
            pool.memset(state[:, 0, :], 0.0).then_inc(const_done, 1)
            pool.wait_ge(const_done, 10)
            pool.affine_select(out=mask4[:, :, :], in_=mask4[:, :, :], compare_op=ALU.is_ge, fill=0.0, base=0,
                               pattern=[[0, 4], [1, P]], channel_multiplier=-1).then_inc(const_done, 1)
            pool.wait_ge(const_done, 11)
            pool.memset(mask4[0:CH, :, CH:P], 0.0).then_inc(const_done, 1)
            pool.memset(reset[:, 0:SEQ:CH], 0.0).then_inc(const_done, 1)
            pool.wait_ge(fin_loaded, 16)
            pool.partition_broadcast(g_fin[:, :], g_fin_row[0:1, :], P).then_inc(fin_bc, 1)

        @block.tensor
        def _(pe):
            pe.sem_inc(y_ready, 1)
            pe.wait_ge(const_done, 6)
            pe.wait_ge(vec_loaded, 96)
            pe.transpose(sc[:, 0:27], vec_rows[:, :], ident[0:27, 0:27]).then_inc(vec_turned, 1)

            for g in range(2):
                for k in range(KT):
                    r = KT * g + k
                    if r >= 2:
                        pe.wait_ge(tr_free, r - 1)
                    if k == 0:
                        pe.wait_ge(x_normed, 4 * g + 4)
                    for t in range(4):
                        mm = pe.transpose(tr[r % 2][:, P * t:P * t + P],
                                          x_t[:, 4 * g + t, P * k:P * k + P], ident[:, :])
                    mm.then_inc(tr_ready, 1)

            def projection(n, slot, c, j_h_k_p):
                h, k, p = j_h_k_p
                if h == 0 and k == 0 and p == 0:
                    pe.wait_ge(lo_done, n + 1)
                if k == 0 and p == 0 and not (isinstance(c, int) and c < 2):
                    pe.wait_ge(proj_free, c - 1)
                mm = pe.matmul(pj[h][:, :], (w_lo if p == 2 else w_hi)[:, slot, k, :],
                               (h_lo if p == 1 else h_hi)[:, k, HALF * h:HALF * h + HALF],
                               start=(k == 0 and p == 0), stop=(k == KT - 1 and p == 2))
                if k == KT - 1 and p == 2:
                    mm.then_inc(proj_ready, 1)

            def whole_tile(n):
                for h in range(2):
                    for k in range(KT):
                        for p in range(3):
                            projection(n, n % 2, bank_no(n) + h, (h, k, p))

            pe.wait_ge(tr_free, R0)
            for n in range(3):
                whole_tile(n)

            def pair(i, tiles):
                plan = plan_projection(tiles)
                for step in range(STEPS):
                    if step < 16:
                        e, qt = step // 8, step % 8
                        if qt == 0:
                            pe.wait_ge(stack_ready, 2 * i + e + 1)
                        pe.wait_ge(sig_done, 16 * i + step + 1)
                        keys = (qt + 1) * P
                        for c0 in range(0, keys, HALF):
                            c1 = min(keys, c0 + HALF)
                            last = c1 == keys
                            lhs = q_st[e][:, P * qt:P * qt + P]
                            pe.matmul(sc[:, c0:c1], lhs, k_hi[e][:, c0:c1], start=True, stop=False)
                            mm = pe.matmul(sc[:, c0:c1], lhs, k_lo[e][:, c0:c1], start=False, stop=not last)
                        mm = pe.matmul(sc[:, keys - P:keys], ident_bf[:, :], mask_neg[:, :],
                                       start=False, stop=True)
                        mm.then_inc(scores_ready, 1)
                    for n, r in enumerate(ROUNDS):
                        if r[0] == "v" and r[1] == step:
                            pe.wait_ge(proj_free, 8 * i + 6)
                            pe.wait_ge(tr_free, RPP * i + R0 + n - 1)
                            for b in range(4):
                                mm = pe.transpose(tr[n % 2][:, P * b:P * b + P],
                                                  v_t[:, P * (4 * r[2] + b):P * (4 * r[2] + b) + P], ident[:, :])
                            mm.then_inc(tr_ready, 1)
                    for j, h, k, p in plan[step]:
                        projection(4 * i + 3 + j, (3 + j) % 2, 8 * i + 6 + 2 * j + h, (h, k, p))
                    if step >= 3 and step % 2:
                        gg = (step - 3) // 2
                        e, g = gg // 4, gg % 4
                        pe.wait_ge(tr_free, RPP * i + R0 + LAST_ROUND[2 * gg + 1] + 1)
                        pe.wait_ge(o_free, 8 * i + gg + 1)
                        blocks = 2 * g + 2
                        for b in range(blocks):
                            c0 = P * max(0, b - 2 * g)
                            for part in (wt_hi, wt_lo):
                                mm = pe.matmul(ob[gg % 2][:, c0:256], v_st[:, e, b, :], part[g % 2][:, b, c0:256],
                                               start=(b == 0 and part is wt_hi),
                                               stop=(b == blocks - 1 and part is wt_lo))
                        mm.then_inc(av_done, 1)
                    for n, r in enumerate(ROUNDS):
                        if r[0] == "w" and r[1] == step:
                            unit, b0, nb = r[2:]
                            pe.wait_ge(w_ready, 16 * i + unit + 1)
                            pe.wait_ge(tr_free, RPP * i + R0 + n - 1)
                            for b in range(nb):
                                mm = pe.transpose(tr[n % 2][:, P * b:P * b + P],
                                                  beta[:, unit % 2, P * (b0 + b):P * (b0 + b) + P], ident[:, :])
                            mm.then_inc(tr_ready, 1)

            with pe.Fori(0, PAIRS - 1) as i:
                pair(i, 4)
            pair(PAIRS - 1, 3)

            for h in range(2):
                pe.wait_ge(proj_free, 36 + h - 1)
                for k in range(KT):
                    for part in (h_hi, h_lo):
                        mm = pe.matmul(pj[h][0:2 * RANK, :], w_lr[:, k, :], part[:, k, HALF * h:HALF * h + HALF],
                                       start=(k == 0 and part is h_hi), stop=(k == KT - 1 and part is h_lo))
                mm.then_inc(proj_ready, 1)

            def v_rounds(hp, j):
                n0 = R3 + R_BODY * hp + 2 * j
                pe.wait_ge(proj_free, bank_no(body_tile(hp, j)) + 2)
                for r in range(2):
                    pe.wait_ge(tr_free, n0 + r - 1)
                    for b in range(4):
                        mm = pe.transpose(tr[(n0 + r) % 2][:, P * b:P * b + P],
                                          gv_t[:, P * (4 * r + b):P * (4 * r + b) + P], ident[:, :])
                    mm.then_inc(tr_ready, 1)

            for hp in range(2):
                q0 = Q_BODY * hp
                for h in range(2):
                    q = q0 + h
                    pe.wait_ge(proj_free, 38)
                    if q >= 4:
                        pe.wait_ge(q4_free, q - 3)
                    else:
                        pe.wait_ge(o_free, 2 + 8 * PAIRS)
                    pe.matmul(ring4[q % 4], w_up[:, P * hp:P * hp + P], lr_t[:, HALF * h:HALF * h + HALF],
                              start=True, stop=True).then_inc(q4_ready, 1)
                for j in range(2):
                    whole_tile(body_tile(hp, j))
                    v_rounds(hp, j)
                pe.wait_ge(dve_step, 7 * hp + 7)
                for r in range(2):
                    n = R3 + R_BODY * hp + 4 + r
                    pe.wait_ge(tr_free, n - 1)
                    for b in range(4):
                        mm = pe.transpose(tr[n % 2][:, P * b:P * b + P], t3[:, P * (4 * r + b):P * (4 * r + b) + P],
                                          ident[:, :])
                    mm.then_inc(tr_ready, 1)
                pe.wait_ge(tr_free, R3 + R_BODY * hp + 6)
                for c in range(NCH - 1):
                    q = q0 + 2 + c
                    if q >= 4:
                        pe.wait_ge(q4_free, q - 3)
                    r0, b = CH * (c % 2), c // 2
                    pe.matmul(ring4[q % 4][:, 0:2 * DV], k_end[r0:r0 + CH, b, :], v_nat[r0:r0 + CH, b, :],
                              start=True, stop=True).then_inc(q4_ready, 1)
                whole_tile(body_tile(hp, 2))
                for r in range(4):
                    q, e, b0 = q0 + 2 + NCH - 1 + r, r % 2, 4 * (r // 2)
                    pe.wait_ge(q4_free, q - 3)
                    for b in range(b0, b0 + 4):
                        mm = pe.matmul(ring4[q % 4][:, P * (b - b0):P * (b - b0) + P],
                                       k_inv[HD * e:HD * e + HD, P * b:P * b + P],
                                       q_dec[HD * e:HD * e + HD, P * b:P * b + P], start=True, stop=True)
                    mm.then_inc(q4_ready, 1)
                for r in range(4):
                    q, e, b0 = q0 + 2 + NCH - 1 + 4 + r, r % 2, 4 * (r // 2)
                    pe.wait_ge(q4_free, q0 + 2 + NCH - 1 + 4)
                    for b in range(b0, b0 + 4):
                        o = ring4[q % 4][:, P * (b - b0):P * (b - b0) + P]
                        pe.matmul(o, sT[:, e, b, :], v_nat[:, b, DV * e:DV * e + DV], start=True, stop=False,
                                  skip_group_check=True)
                        for cc in range(2):
                            s0 = P * b + CH * cc
                            mm = pe.matmul(o[CH * cc:CH * cc + CH, :], q_dec[HD * e:HD * e + HD, s0:s0 + CH],
                                           state[HD * e:HD * e + HD, 2 * b + cc, :], start=False, stop=(cc == 1),
                                           skip_group_check=True)
                    mm.then_inc(q4_ready, 1)
                for j in range(3, len(BODY[hp])):
                    whole_tile(body_tile(hp, j))
                pe.wait_ge(rstd_ready, 2 + 2 * hp + 2)
                for r in range(4):
                    n, e, half = R3 + R_BODY * hp + 6 + r, r // 2, r % 2
                    pe.wait_ge(tr_free, n - 1)
                    for b in range(4):
                        mm = pe.transpose(tr[n % 2][:, P * b:P * b + P], o_nat[:, e, 4 * half + b, :], ident[:, :])
                    mm.then_inc(tr_ready, 1)

            pe.wait_ge(proj_free, bank_no(N4))
            pe.wait_ge(q4_free, 2 * Q_BODY)
            with pe.Fori(0, KT // 2) as jj:
                for u in range(2):
                    n = 6 * jj + N4 + 3 * u
                    for g in range(2):
                        slot = (N4 + 3 * u + g) % 2
                        pe.wait_ge(lo_done, n + g + 1)
                        for h in range(2):
                            c = 8 * jj + 4 * u + 2 * g + h
                            pe.wait_ge(gate_free, c + 1)
                            for k in range(KT):
                                for p in range(3):
                                    mm = pe.matmul(pj[h][:, :], (w_lo if p == 2 else w_hi)[:, slot, k, :],
                                                   (h_lo if p == 1 else h_hi)[:, k, HALF * h:HALF * h + HALF],
                                                   start=(k == 0 and p == 0), stop=(k == KT - 1 and p == 2))
                            mm.then_inc(gate_ready, 1)
                    slot = (N4 + 3 * u + 2) % 2
                    pe.wait_ge(lo_done, n + 3)
                    pe.wait_ge(gs_lo, 8)
                    for h in range(2):
                        for br in range(2):
                            pe.wait_ge(y_free, 8 * jj + 4 * u + 2 * h + br + 1)
                            for k in range(4 * br, 4 * br + 4):
                                for p in range(3):
                                    mm = pe.matmul(ring4[2 * h + br], (w_lo if p == 2 else w_hi)[:, slot, k, :],
                                                   (g_lo if p == 1 else g_hi)[:, k, HALF * h:HALF * h + HALF],
                                                   start=(k == 4 * br and p == 0), stop=(k == 4 * br + 3 and p == 2))
                            mm.then_inc(y_ready, 1)

            pe.wait_ge(y_free, 4 + 4 * KT)
            for t in range(ST):
                slot = (N5 + t) % 2
                pe.wait_ge(lo_done, N5 + t + 1)
                for e in range(2):
                    c = 2 * t + e
                    if c >= 4:
                        pe.wait_ge(o5_free, c - 3)
                    for k in range(KT):
                        if t == 0 and k % 4 == 0:
                            pe.wait_ge(wout_l, 2 * e + k // 4 + 1)
                        for p in range(3):
                            mm = pe.matmul(ring4[c % 4], (w_lo if p == 2 else w_hi)[:, slot, k, :],
                                           (wout_lo if p == 1 else wout_hi)[e][:, k, :],
                                           start=(k == 0 and p == 0), stop=(k == KT - 1 and p == 2))
                    mm.then_inc(o5_ready, 1)

        @block.scalar
        def _(act):
            act.sem_inc(sig_done, 1)
            act.sem_inc(gate_free, 2)
            act.wait_ge(const_done, 1)
            act.wait_ge(cols_ready, 1)
            for g in range(2):
                for t in range(4 * g, 4 * g + 4):
                    act.wait_ge(x_loaded[t], 16)
                    if t:
                        act.wait_ge(sq_done, t + g)
                    act.activation(junk[:, :], x_t[:, t, :], ACT.Square, accum_out=stats[:, t:t + 1])\
                        .then_inc(sq_done, 1)
                act.wait_ge(sq_done, 5 * g + 4)
                act.activation(stats[:, 8 + 4 * g:12 + 4 * g], stats[:, 4 * g:4 * g + 4], ACT.Sqrt,
                               bias=stats[:, 63:64], scale=1.0 / D).then_inc(sq_done, 1)
            act.wait_ge(lr_loaded, 16)
            act.activation(w_lr[:, :, 0:RANK], lr_raw[:, :, :], ACT.Copy).then_inc(lr_split, 1)

            act.wait_ge(cols_ready, 2)
            for g in range(2):
                for k in range(KT):
                    r = KT * g + k
                    act.wait_ge(tr_ready, r + 1)
                    act.activation(h_hi[:, k, HALF * g:HALF * g + HALF], tr[r % 2][:, :], ACT.Copy,
                                   scale=cols[:, k:k + 1]).then_inc(tr_act, 1)
                if g == 0:
                    act.wait_ge(raw_loaded[0], 16)
                    act.activation(w_hi[:, 0, :, :], w_raw[:, 0, :, :], ACT.Copy).then_inc(hi_done, 1)

            def high_part(n, slot, loads, done_sem, done):
                act.wait_ge(raw_loaded[slot], 16 * loads)
                if done is not None:
                    act.wait_ge(done_sem, done)
                act.activation(w_hi[:, slot, :, :], w_raw[:, slot, :, :], ACT.Copy).then_inc(hi_done, 1)

            def stage(dst, c, h):
                act.wait_ge(proj_ready, c + 1)
                act.activation(dst[:, HALF * h:HALF * h + 256], pj[h][:, 0:256], ACT.Copy).then_inc(proj_act, 1)

            def build_stack(e, head, staged):
                act.wait_ge(proj_free, staged)
                own, other = slice(HD * e, HD * e + HD), slice(HD * (1 - e), HD * (1 - e) + HD)
                act.activation(q_st[e][own, :], stage_q[own, :], ACT.Copy)
                act.activation(k_hi[e][own, :], stage_k[own, :], ACT.Copy)
                act.activation(k_hi[e][other, :], stage_k[own, :], ACT.Copy).then_inc(stack_hi, 1)

            for n, dst in enumerate((stage_q, stage_k, v_t)):
                stage(dst, 2 * n, 0)
                high_part(n + 1, (n + 1) % 2, (n + 1) // 2 + 1, proj_ready, 2 * n if n else None)
                stage(dst, 2 * n + 1, 1)
            build_stack(0, 0, 4)

            def pair(i, tiles, last):
                plan = plan_projection(tiles)
                dsts = [None, stage_q, stage_k, v_t]
                for step in range(STEPS):
                    if step < 16:
                        keys = (step % 8 + 1) * P
                        act.wait_ge(scores_ready, 16 * i + step + 1)
                        act.activation(surv[:, step % 2, 0:keys], sc[:, 0:keys], ACT.Sigmoid, scale=-HD ** -0.5)
                        act.activation(beta[:, step % 2, 0:keys], sc[:, 0:keys], ACT.Sigmoid, scale=HD ** -0.5)\
                            .then_inc(sig_done, 1)
                    for n, r in enumerate(ROUNDS):
                        if r[0] == "v" and r[1] == step:
                            act.wait_ge(tr_ready, RPP * i + R0 + n + 1)
                            act.activation(v_st[:, :, 4 * r[2]:4 * r[2] + 4, 0:HD],
                                           tr[n % 2][:, :].rearrange("p (b e d) -> p e b d", d=HD, e=2),
                                           ACT.Copy).then_inc(tr_act, 1)
                    if step == 1:
                        build_stack(1, None, 8 * i + 4)
                    for j, h, k, p in plan[step]:
                        if k < KT - 1 or p < 2:
                            continue
                        c = 8 * i + 6 + 2 * j + h
                        if h == 0 and not (last and j == tiles - 1):
                            high_part(None, j % 2, 2 * i + 3 + j // 2, proj_ready, 8 * i + 6 + 2 * j)
                        if j == 0:
                            act.wait_ge(proj_ready, c + 1)
                            if h == 1:
                                act.wait_ge(proj_free, c)
                            act.activation(z_sig[:, :], pj[h][:, :], ACT.Sigmoid).then_inc(proj_act, 1)
                        else:
                            act.wait_ge(stack_ready, 2 * i + 2)
                            stage(dsts[j], c, h)
                        if j == 2 and h == 1 and not last:
                            build_stack(0, None, 8 * i + 12)
                    if step >= 3 and step % 2:
                        gg = (step - 3) // 2
                        e = gg // 4
                        act.wait_ge(av_done, 8 * i + gg + 1)
                        act.activation(o_low[HD * e:HD * e + HD, gg % 2, :], ob[gg % 2][HD:P, 0:256],
                                       ACT.Copy).then_inc(o_copied, 1)
                    for n, r in enumerate(ROUNDS):
                        if r[0] == "w" and r[1] == step:
                            unit, b0, nb = r[2:]
                            g = unit % 8 // 2
                            act.wait_ge(tr_ready, RPP * i + R0 + n + 1)
                            act.activation(wt_hi[g % 2][:, b0:b0 + nb, P * (unit % 2):P * (unit % 2) + P],
                                           tr[n % 2][:, 0:P * nb].rearrange("p (b q) -> p b q", q=P),
                                           ACT.Copy).then_inc(tr_act, 1)

            with act.Fori(0, PAIRS - 1) as i:
                pair(i, 4, False)
            pair(PAIRS - 1, 3, True)

            act.wait_ge(o_free, 2 + 8 * PAIRS)
            act.wait_ge(g_done, 8 * PAIRS)
            for h in range(2):
                act.wait_ge(proj_ready, 36 + h + 1)
                act.activation(lr_t[:, HALF * h:HALF * h + 256], pj[h][0:2 * RANK, 0:256], ACT.Copy)\
                    .then_inc(proj_act, 1)

            def gz_sigmoid(c, h):
                act.wait_ge(proj_ready, c + 1)
                act.wait_ge(proj_free, c)
                act.activation(gz_sig[:, :], pj[h][:, :], ACT.Sigmoid).then_inc(proj_act, 1)

            def body_evacuate(hp, j):
                n = body_tile(hp, j)
                kind, m = BODY[hp][j]
                for h in range(2):
                    c = bank_no(n) + h
                    if kind == "z":
                        gz_sigmoid(c, h)
                    elif kind == "v":
                        stage(gv_t, c, h)
                    else:
                        stage(stage_q if kind == "q" else stage_k, c, h)
                    if h == 0:
                        m1 = n + 1
                        high_part(m1, m1 % 2, m1 // 2 + 1, proj_ready, bank_no(m1 - 2) + 2)

            def copy_round(n, dst):
                act.wait_ge(tr_ready, n + 1)
                act.activation(dst, tr[n % 2][:, 0:256].rearrange("p (b d) -> p b d", d=P), ACT.Copy)\
                    .then_inc(tr_act, 1)

            high_part(18, 0, 10, proj_ready, bank_no(16) + 2)
            t1, t2 = t12[:, 0, :], t12[:, 1, :]
            for hp in range(2):
                q0, s0, d0, r0 = Q_BODY * hp, 5 * hp, 7 * hp, R3 + R_BODY * hp
                bias = cols[:, 24 + hp:25 + hp]
                if hp:
                    act.wait_ge(tr_ready, r0)
                for h in range(2):
                    act.wait_ge(q4_ready, q0 + h + 1)
                    act.activation(t1[:, HALF * h:HALF * h + HALF], ring4[(q0 + h) % 4], ACT.Abs,
                                   bias=bias).then_inc(q4_act, 1)
                act.wait_ge(q4_act, (2 + 4) * hp + 2)
                act.activation(t1, t1, ACT.Exp, scale=-1.0).then_inc(act_step, 1)
                act.wait_ge(act_step, s0 + 1)
                act.activation(t1, t1, ACT.Ln, bias=1.0).then_inc(act_step, 1)
                act.wait_ge(dve_step, d0 + 2)
                act.activation(t2, t1, ACT.Exp, scale=1.0 / 16).then_inc(act_step, 1)
                act.activation(t3[:, :], t1, ACT.Exp, scale=-1.0 / 16).then_inc(act_step, 1)
                act.wait_ge(dve_step, d0 + 6)
                act.activation(t2, t2, ACT.Exp, scale=1.0 / 16).then_inc(act_step, 1)
                for j in range(2):
                    body_evacuate(hp, j)
                    for r in range(2):
                        copy_round(r0 + 2 * j + r, v_nat[:, 4 * r:4 * r + 2, DV * j:DV * j + DV])
                for r in range(2):
                    copy_round(r0 + 4 + r, k_end[:, 4 * r:4 * r + 2, :])
                body_evacuate(hp, 2)
                for r in range(4):
                    q, e, b0 = q0 + 2 + NCH - 1 + 4 + r, r % 2, 4 * (r // 2)
                    act.wait_ge(q4_ready, q + 1)
                    if r >= 2:
                        act.wait_ge(q4_act, 6 * hp + 2 + r - 1)
                    for b in range(4):
                        sq = P * (4 * (r % 2) + b)
                        a = act.activation(t3[:, sq:sq + P], ring4[q % 4][:, P * b:P * b + P], ACT.Square,
                                           accum_out=stats[:, 16 + 8 * e + b0 + b:17 + 8 * e + b0 + b])
                    a.then_inc(q4_act, 1)
                act.wait_ge(q4_act, 6 * hp + 6)
                act.activation(stats[:, 32:48], stats[:, 16:32], ACT.Sqrt, bias=stats[:, 63:64],
                               scale=1.0 / DV).then_inc(sq_done, 1)
                for j in range(3, len(BODY[hp])):
                    body_evacuate(hp, j)

            act.wait_ge(tr_free, R3 + 2 * R_BODY)
            def split_g(k):
                act.activation(g_hi[:, k, :], G[:, k, :], ACT.Copy).then_inc(gs_hi, 1)

            for k in range(8):
                split_g(k)
            def gates(jj, last):
                for u in range(2):
                    for g in range(2):
                        act.activation(gate_bias[:, u, g:g + 1], cols[:, bass.ds(2 * jj + 8 + 8 * g + u, 1)],
                                       ACT.Copy).then_inc(bias_ready, 1)
                    for g in range(2):
                        for h in range(2):
                            c = 8 * jj + 4 * u + 2 * g + h
                            if g == 0 and h == 0:
                                act.wait_ge(bias_ready, 4 * jj + 2 * u + 2)
                            act.wait_ge(gate_ready, c + 1)
                            if g == 0 and h == 0:
                                act.wait_ge(y_free, 8 * jj + 4 * u + 4)
                            act.activation(gate[:, g, HALF * h:HALF * h + HALF], pj[h][:, :], ACT.Sigmoid,
                                           bias=gate_bias[:, u, g:g + 1]).then_inc(gate_free, 1)
                            if h == 0 and g == 0:
                                slot = (N4 + 3 * u + 1) % 2
                                high_part(None, slot, 3 * jj + (N4 + 3 * u + 1) // 2 + 1, y_ready,
                                          8 * jj + 4 * u + 1)
                            if h == 0 and g == 1:
                                slot = (N4 + 3 * u + 2) % 2
                                act.wait_ge(lr_loaded, 32 * jj + 16 * u + 32)
                                high_part(None, slot, 3 * jj + (N4 + 3 * u + 2) // 2 + 1, gate_ready,
                                          8 * jj + 4 * u + 2)
                    slot = (N4 + 3 * u + 3) % 2
                    if u == 0:
                        high_part(None, slot, 3 * jj + (N4 + 3) // 2 + 1, gate_ready, 8 * jj + 4)
                    elif not last:
                        high_part(None, slot, 3 * jj + (N4 + 6) // 2 + 1, gate_ready, 8 * jj + 8)

            with act.Fori(0, KT // 2 - 1) as jj:
                gates(jj, False)
            gates(KT // 2 - 1, True)

            def split_m(t):
                slot = (N5 + t) % 2
                act.wait_ge(m_ready, 2 * KT)
                if t >= 2:
                    act.wait_ge(o5_ready, 2 * (t - 2) + 2)
                else:
                    act.wait_ge(y_ready, 1 + 4 * KT)
                act.activation(w_hi[:, slot, :, :], mT[:, :, P * t:P * t + P], ACT.Copy).then_inc(hi_done, 1)

            for e in range(2):
                if e == 1:
                    split_m(0)
                for c in (2 * e, 2 * e + 1):
                    kk = 4 * (c % 2)
                    act.wait_ge(wout_loaded[c], 16)
                    act.activation(wout_hi[e][:, kk:kk + 4, :],
                                   wout_raw[:, kk:kk + 4, HALF * e:HALF * e + HALF], ACT.Copy).then_inc(wout_h, 1)
            for t in range(ST):
                if t + 1 < ST:
                    split_m(t + 1)
                act.wait_ge(o5_free, 2 * t + 2)
                act.activation(junk5[:, :], y_row[:, t % 2, :], ACT.Square, accum_out=stats[:, 48 + t % 2:49 + t % 2])\
                    .then_inc(ss5, 1)
                act.wait_ge(ss5, 2 * t + 1)
                act.activation(stats[:, 50 + t % 2:51 + t % 2], stats[:, 48 + t % 2:49 + t % 2], ACT.Sqrt,
                               bias=stats[:, 63:64], scale=1.0 / D).then_inc(ss5, 1)

        @block.vector
        def _(dve):
            dve.sem_inc(o_free, 2)
            dve.sem_inc(y_free, 4)
            dve.memset(stats[:, 63:64], EPS).then_inc(cols_ready, 1)
            dve.wait_ge(vec_turned, 1)
            dve.tensor_copy(cols[:, :], sc[:, 0:27]).then_inc(cols_ready, 1)
            for g in range(2):
                dve.wait_ge(sq_done, 5 * g + 5)
                dve.reciprocal(stats[:, 8 + 4 * g:12 + 4 * g], stats[:, 8 + 4 * g:12 + 4 * g]).then_inc(rstd_ready, 1)
                dve.wait_ge(rstd_ready, g + 1)
                for t in range(4 * g, 4 * g + 4):
                    dve.tensor_scalar(x_t[:, t, :], x_t[:, t, :], stats[:, 8 + t:9 + t], None, ALU.mult)\
                        .then_inc(x_normed, 1)
            dve.wait_ge(lr_split, 1)
            dve.tensor_tensor(w_lr[:, :, RANK:2 * RANK], lr_raw[:, :, :], w_lr[:, :, 0:RANK].bitcast(F32),
                              ALU.subtract).then_inc(lr_split, 1)

            def low_part(n, slot):
                dve.wait_ge(hi_done, n + 1)
                dve.tensor_tensor(w_lo[:, slot, :, :], w_raw[:, slot, :, :], w_hi[:, slot, :, :].bitcast(F32),
                                  ALU.subtract).then_inc(lo_done, 1)

            dve.wait_ge(cols_ready, 2)
            for g in range(2):
                for k in range(KT):
                    r = KT * g + k
                    hs = slice(HALF * g, HALF * g + HALF)
                    dve.wait_ge(tr_act, r + 1)
                    dve.scalar_tensor_tensor(out=h_lo[:, k, hs], in0=tr[r % 2][:, :], scalar=cols[:, k:k + 1],
                                             in1=h_hi[:, k, hs].bitcast(F32), op0=ALU.mult, op1=ALU.subtract)\
                        .then_inc(tr_free, 1)
                if g == 0:
                    low_part(0, 0)
            dve.memset(surv[:, :, :], 1.0).then_inc(cols_ready, 1)
            dve.wait_ge(cols_ready, 3)

            def stage(dst, c, h):
                dve.wait_ge(proj_act, c + 1)
                dve.tensor_copy(dst[:, HALF * h + 256:HALF * h + HALF], pj[h][:, 256:HALF]).then_inc(proj_free, 1)

            def build_stack(e, head, staged):
                own, other = slice(HD * e, HD * e + HD), slice(HD * (1 - e), HD * (1 - e) + HD)
                dve.wait_ge(proj_free, staged)
                dve.wait_ge(stack_hi, head + 1)
                dve.tensor_tensor(q_st[e][other, :], stage_q[own, :], q_st[e][own, :].bitcast(F32), ALU.subtract)
                dve.tensor_tensor(k_lo[e][own, :], stage_k[own, :], k_hi[e][own, :].bitcast(F32), ALU.subtract)
                dve.tensor_tensor(k_lo[e][other, :], stage_k[own, :], k_hi[e][own, :].bitcast(F32), ALU.subtract)\
                    .then_inc(stack_ready, 1)

            for n, dst in enumerate((stage_q, stage_k, v_t)):
                stage(dst, 2 * n, 0)
                low_part(n + 1, (n + 1) % 2)
                stage(dst, 2 * n + 1, 1)
            build_stack(0, 0, 4)

            def pair(i, tiles, last):
                plan = plan_projection(tiles)
                dsts = [None, stage_q, stage_k, v_t]
                for step in range(STEPS):
                    if step < 16:
                        keys = (step % 8 + 1) * P
                        s = surv[:, step % 2, 0:keys]
                        dve.wait_ge(sig_done, 16 * i + step + 2)
                        dve.tensor_tensor_scan(s[:, ::-1], s[:, ::-1], s[:, ::-1], 1.0, ALU.mult, ALU.bypass)\
                            .then_inc(scan_done, 1)
                        dve.wait_ge(scan_done, 16 * i + step + 1)
                        dve.tensor_tensor(beta[:, step % 2, 0:keys], beta[:, step % 2, 0:keys],
                                          surv[:, step % 2, 1:keys + 1], ALU.mult).then_inc(w_ready, 1)
                    for n, r in enumerate(ROUNDS):
                        if r[0] == "v" and r[1] == step:
                            dve.wait_ge(tr_act, RPP * i + R0 + n + 1)
                            vb = slice(4 * r[2], 4 * r[2] + 4)
                            dve.tensor_tensor(v_st[:, :, vb, HD:P],
                                              tr[n % 2][:, :].rearrange("p (b e d) -> p e b d", d=HD, e=2),
                                              v_st[:, :, vb, 0:HD].bitcast(F32), ALU.subtract).then_inc(tr_free, 1)
                    if step == 1:
                        build_stack(1, 2 * i + 1, 8 * i + 4)
                    for j, h, k, p in plan[step]:
                        if k < KT - 1 or p < 2:
                            continue
                        c = 8 * i + 6 + 2 * j + h
                        if h == 0 and not (last and j == tiles - 1):
                            low_part(4 * i + 4 + j, j % 2)
                        if j == 0:
                            dve.wait_ge(proj_act, c + 1)
                            dve.tensor_tensor(z_silu[:, HALF * h:HALF * h + HALF], pj[h][:, :], z_sig[:, :],
                                              ALU.mult).then_inc(proj_free, 1)
                        else:
                            stage(dsts[j], c, h)
                        if j == 2 and h == 1 and not last:
                            build_stack(0, 2 * i + 2, 8 * i + 12)
                    if step >= 3 and step % 2:
                        gg = (step - 3) // 2
                        e, g = gg // 4, gg % 4
                        own = slice(HD * e, HD * e + HD)
                        low = o_low[own, gg % 2, :]
                        dve.wait_ge(o_copied, 8 * i + gg + 1)
                        dve.tensor_tensor(low, ob[gg % 2][0:HD, 0:256], low, ALU.add).then_inc(o_free, 1)
                        dve.wait_ge(o_free, 8 * i + gg + 3)
                        dve.wait_ge(proj_free, 8 * i + 7 + g // 2)
                        dve.tensor_tensor(G[own, bass.ds(i, 1), 256 * g:256 * g + 256].rearrange("p a c -> p (a c)"),
                                          low, z_silu[own, 256 * g:256 * g + 256], ALU.mult).then_inc(g_done, 1)
                    for n, r in enumerate(ROUNDS):
                        if r[0] == "w" and r[1] == step:
                            unit, b0, nb = r[2:]
                            g = unit % 8 // 2
                            qs = slice(P * (unit % 2), P * (unit % 2) + P)
                            dve.wait_ge(tr_act, RPP * i + R0 + n + 1)
                            dve.tensor_tensor(wt_lo[g % 2][:, b0:b0 + nb, qs],
                                              tr[n % 2][:, 0:P * nb].rearrange("p (b q) -> p b q", q=P),
                                              wt_hi[g % 2][:, b0:b0 + nb, qs].bitcast(F32),
                                              ALU.subtract).then_inc(tr_free, 1)

            with dve.Fori(0, PAIRS - 1) as i:
                pair(i, 4, False)
            pair(PAIRS - 1, 3, True)

            for h in range(2):
                dve.wait_ge(proj_act, 36 + h + 1)
                dve.tensor_copy(lr_t[:, HALF * h + 256:HALF * h + HALF], pj[h][0:2 * RANK, 256:HALF])\
                    .then_inc(proj_free, 1)

            def body_evacuate(hp, j):
                n = body_tile(hp, j)
                kind, m = BODY[hp][j]
                for h in range(2):
                    c = bank_no(n) + h
                    if kind == "z":
                        dve.wait_ge(proj_act, c + 1)
                        dve.tensor_tensor(gz[:, m % 2, HALF * h:HALF * h + HALF], pj[h][:, :], gz_sig[:, :],
                                          ALU.mult).then_inc(proj_free, 1)
                    elif kind == "v":
                        stage(gv_t, c, h)
                    else:
                        stage(stage_q if kind == "q" else stage_k, c, h)
                    if h == 0:
                        low_part(n + 1, (n + 1) % 2)

            def copy_round(n, act_no, dst):
                dve.wait_ge(tr_act, act_no + 1)
                dve.tensor_copy(dst, tr[n % 2][:, 256:HALF].rearrange("p (b d) -> p b d", d=P)).then_inc(tr_free, 1)

            low_part(18, 0)
            t1, t2 = t12[:, 0, :], t12[:, 1, :]
            by_chunk = t1.rearrange("p (c s) -> p c s", s=CH)
            for hp in range(2):
                q0, s0, d0, r0 = Q_BODY * hp, 5 * hp, 7 * hp, R3 + R_BODY * hp
                a0 = R3 + 6 * hp
                bias = cols[:, 24 + hp:25 + hp]
                for h in range(2):
                    dve.wait_ge(q4_act, 6 * hp + h + 1)
                    dve.tensor_scalar(t2[:, HALF * h:HALF * h + HALF], ring4[(q0 + h) % 4], bias, 0.0,
                                      ALU.add, ALU.min).then_inc(q4_free, 1)
                dve.wait_ge(q4_free, q0 + 2)
                dve.wait_ge(act_step, s0 + 2)
                dve.tensor_tensor(t2, t2, t1, ALU.subtract).then_inc(dve_step, 1)
                dve.wait_ge(dve_step, d0 + 1)
                dve.wait_ge(const_done, 13)
                dve.tensor_tensor_scan(t1, reset[:, :], t2, 0.0, ALU.mult, ALU.add).then_inc(dve_step, 1)
                dve.wait_ge(act_step, s0 + 3)
                dve.scalar_tensor_tensor(out=q_dec[:, :], in0=stage_q[:, :], scalar=HD ** -0.5, in1=t2,
                                         op0=ALU.mult, op1=ALU.mult).then_inc(dve_step, 1)
                dve.tensor_copy(stats[:, 48:48 + NCH - 1], t2[:, CH - 1:SEQ - CH:CH]).then_inc(dve_step, 1)
                dve.wait_ge(act_step, s0 + 4)
                dve.tensor_tensor(k_inv[:, :], stage_k[:, :], t3[:, :], ALU.mult).then_inc(dve_step, 1)
                dve.wait_ge(dve_step, d0 + 4)
                dve.tensor_tensor(t2.rearrange("p (c s) -> p c s", s=CH),
                                  by_chunk[:, :, CH - 1:CH].to_broadcast([P, NCH, CH]), by_chunk,
                                  ALU.subtract).then_inc(dve_step, 1)
                dve.wait_ge(act_step, s0 + 5)
                dve.wait_ge(dve_step, d0 + 6)
                dve.tensor_tensor(t3[:, :], stage_k[:, :], t2, ALU.mult).then_inc(dve_step, 1)
                for j in range(2):
                    body_evacuate(hp, j)
                    for r in range(2):
                        copy_round(r0 + 2 * j + r, a0 + 2 * j + r, v_nat[:, 4 * r + 2:4 * r + 4, DV * j:DV * j + DV])
                for r in range(2):
                    copy_round(r0 + 4 + r, a0 + 4 + r, k_end[:, 4 * r + 2:4 * r + 4, :])
                for c in range(NCH - 1):
                    q = q0 + 2 + c
                    dec = stats[:, 48 + c:49 + c]
                    dve.wait_ge(q4_ready, q + 1)
                    if c:
                        dve.wait_ge(q4_free, q)
                    for e in range(2):
                        own = slice(HD * e, HD * e + HD)
                        ins = dve.scalar_tensor_tensor(out=state[own, c + 1, :], in0=state[own, c, :],
                                                       scalar=dec[own, :], in1=ring4[q % 4][own, DV * e:DV * e + DV],
                                                       op0=ALU.mult, op1=ALU.add)
                    ins.then_inc(q4_free, 1)
                body_evacuate(hp, 2)
                for r in range(4):
                    q, e, b0 = q0 + 2 + NCH - 1 + r, r % 2, 4 * (r // 2)
                    dve.wait_ge(q4_ready, q + 1)
                    dve.copy_predicated(sT[:, e, b0:b0 + 4, :], mask4[:, :, :].bitcast(I32),
                                        ring4[q % 4].rearrange("p (b q) -> p b q", q=P)).then_inc(q4_free, 1)
                for r in range(4):
                    q, e, b0 = q0 + 2 + NCH - 1 + 4 + r, r % 2, 4 * (r // 2)
                    dve.wait_ge(q4_act, 6 * hp + 2 + r + 1)
                    dve.tensor_copy(o_nat[:, e, b0:b0 + 4, :], ring4[q % 4].rearrange("p (b q) -> p b q", q=P))\
                        .then_inc(q4_free, 1)
                dve.wait_ge(sq_done, 10 + hp + 1)
                dve.reciprocal(stats[:, 32:48], stats[:, 32:48]).then_inc(rstd_ready, 1)
                dve.wait_ge(rstd_ready, 2 + 2 * hp + 1)
                o_flat = o_nat.rearrange("p e b q -> p (e b) q")
                dve.wait_ge(q4_free, Q_BODY * (hp + 1))
                dve.tensor_tensor(o_flat, o_flat,
                                  stats[:, 32:48].rearrange("p (a b) -> p a b", b=1).to_broadcast([P, 16, P]),
                                  ALU.mult).then_inc(rstd_ready, 1)
                for j in range(3, len(BODY[hp])):
                    body_evacuate(hp, j)
                dve.wait_ge(proj_free, bank_no(body_tile(hp, 3)) + 2)
                for r in range(4):
                    n, e, half = r0 + 6 + r, r // 2, r % 2
                    hs = slice(HALF * half, HALF * half + HALF)
                    dve.wait_ge(tr_ready, n + 1)
                    dve.scalar_tensor_tensor(out=G[:, 4 + 2 * hp + e, hs], in0=tr[n % 2][:, :], scalar=cols[:, 26:27],
                                             in1=gz[:, e, hs], op0=ALU.mult, op1=ALU.mult).then_inc(tr_free, 1)

            dve.wait_ge(tr_free, R3 + 2 * R_BODY)
            for k in range(8):
                dve.wait_ge(gs_hi, k + 1)
                dve.tensor_tensor(g_lo[:, k, :], G[:, k, :], g_hi[:, k, :].bitcast(F32), ALU.subtract)\
                    .then_inc(gs_lo, 1)
            def gates(jj, last):
                for u in range(2):
                    n = 6 * jj + N4 + 3 * u
                    low_part(n + 1, (N4 + 3 * u + 1) % 2)
                    low_part(n + 2, (N4 + 3 * u + 2) % 2)
                    if u == 0:
                        low_part(n + 3, (N4 + 3) % 2)
                    elif not last:
                        low_part(n + 3, (N4 + 6) % 2)
                    dve.wait_ge(gate_free, 8 * jj + 4 * u + 4 + 2)
                    for h in range(2):
                        for br in range(2):
                            c = 8 * jj + 4 * u + 2 * h + br
                            dve.wait_ge(y_ready, c + 2)
                            dve.tensor_tensor(y_g[:, h, br, :], ring4[2 * h + br], gate[:, br, HALF * h:HALF * h + HALF],
                                              ALU.mult).then_inc(y_free, 1)
                        dve.wait_ge(y_free, 8 * jj + 4 * u + 2 * h + 2 + 4)
                        dve.tensor_tensor(
                            mT[:, bass.ds(2 * jj + u, 1), HALF * h:HALF * h + HALF].rearrange("p a c -> p (a c)"),
                            y_g[:, h, 0, :], y_g[:, h, 1, :], ALU.add).then_inc(m_ready, 1)

            with dve.Fori(0, KT // 2 - 1) as jj:
                gates(jj, False)
            gates(KT // 2 - 1, True)

            def split_m(t):
                slot = (N5 + t) % 2
                dve.wait_ge(m_ready, 2 * KT)
                dve.wait_ge(hi_done, N5 + t + 1)
                dve.tensor_tensor(w_lo[:, slot, :, :], mT[:, :, P * t:P * t + P], w_hi[:, slot, :, :].bitcast(F32),
                                  ALU.subtract).then_inc(lo_done, 1)

            for c in range(4):
                e, kk = c // 2, 4 * (c % 2)
                if c == 2:
                    split_m(0)
                dve.wait_ge(wout_h, c + 1)
                dve.tensor_tensor(wout_lo[e][:, kk:kk + 4, :], wout_raw[:, kk:kk + 4, HALF * e:HALF * e + HALF],
                                  wout_hi[e][:, kk:kk + 4, :].bitcast(F32), ALU.subtract).then_inc(wout_l, 1)
            dve.wait_ge(fin_bc, 1)
            for t in range(ST):
                if t + 1 < ST:
                    split_m(t + 1)
                dve.wait_ge(xr_loaded[t % 2], 16 * (t // 2 + 1))
                for e in range(2):
                    c = 2 * t + e
                    es = slice(HALF * e, HALF * e + HALF)
                    dve.wait_ge(o5_ready, c + 1)
                    dve.tensor_tensor(y_row[:, t % 2, es], ring4[c % 4], x_res[:, t % 2, es], ALU.add)\
                        .then_inc(o5_free, 1)
                dve.wait_ge(ss5, 2 * t + 2)
                dve.reciprocal(stats[:, 52 + t % 2:53 + t % 2], stats[:, 50 + t % 2:51 + t % 2]).then_inc(rstd5, 1)
                dve.wait_ge(rstd5, t + 1)
                if t >= 2:
                    dve.wait_ge(stored[t % 2], 16 * (t // 2))
                dve.scalar_tensor_tensor(out=y_out[:, t % 2, :], in0=y_row[:, t % 2, :],
                                         scalar=stats[:, 52 + t % 2:53 + t % 2], in1=g_fin[:, :],
                                         op0=ALU.mult, op1=ALU.mult).then_inc(y_done, 1)


_INS = ["x", "g_pre", "w_in", "b_gate", "w_alpha_up", "b_alpha_up", "g_gla_norm",
        "w_o_sb", "w_o_gla", "w_out", "g_final"]


def kernel(**inputs):
    import numpy as np
    import concourse.bacc as bacc
    from concourse.bass_utils import run_bass_kernel_spmd

    nc = bacc.Bacc("TRN2", target_bir_lowering=False, num_devices=1)
    arrays, args = {}, []
    for name in _INS:
        a = np.ascontiguousarray(inputs[name])
        arrays[f"in_{name}"] = a
        args.append(nc.dram_tensor(f"in_{name}", a.shape, mybir.dt.from_np(a.dtype), kind="ExternalInput").ap())
    args.append(nc.dram_tensor("out_y", (1, SEQ, D), F32, kind="ExternalOutput").ap())
    stickbreak_gla_hybrid(nc, *args)
    r = run_bass_kernel_spmd(nc, [arrays], core_ids=[0])
    return r.results[0]["out_y"]
```

```python
from contextlib import ExitStack

import concourse.bass as bass
from concourse import mybir

ALU = mybir.AluOpType
ACT = mybir.ActivationFunctionType
F32 = mybir.dt.float32
F32R = mybir.dt.float32r
BF16 = mybir.dt.bfloat16
I32 = mybir.dt.int32

P = 128
HALF = 512
NEG = -1.0e30
EPS = 1e-6

D = 1024
SEQ = 1024
SBW = D // 2
HD = 64
GKW = D // 4
GVW = D // 2
DV = 128
CH = 64
RANK = 16
KT = D // P
ST = SEQ // P
PAIRS = SBW // P
NCH = SEQ // CH

COL_Q, COL_K, COL_V, COL_Z = 0, SBW, 2 * SBW, 3 * SBW
COL_GQ = 4 * SBW
COL_GK = COL_GQ + GKW
COL_GV = COL_GK + GKW
COL_GZ = COL_GV + GVW
COL_LR = COL_GZ + GVW
COL_GA = COL_LR + RANK
COL_GB = COL_GA + D

MM_HALF = KT * 3
STEPS = 18
SHARE = [13, 12, 11, 11, 11, 11, 11, 12] + [8, 8, 8, 9, 9, 10, 12, 16] + [10, 10]
assert sum(SHARE) == 8 * MM_HALF
STACK_STEPS = (9, 14, 17)
SECOND_STEPS = (1, 3, 4)
assert sum(SHARE[:STACK_STEPS[0]]) >= 4 * MM_HALF and sum(SHARE[:STACK_STEPS[1]]) >= 6 * MM_HALF


def plan_projection():
    work = [(j, h, k, p) for j in range(4) for h in range(2) for k in range(KT) for p in range(3)]
    steps, at = [], 0
    for share in SHARE:
        steps.append(work[at:at + share])
        at += share
    return steps


def plan_rounds():
    rounds = []
    for step in range(STEPS):
        if step in (1, 2):
            rounds.append(("v", step, step - 1))
        if 1 <= step <= 16:
            unit = step - 1
            blocks = unit % 8 + 1
            for b in range(0, blocks, 4):
                rounds.append(("w", step, unit, b, min(4, blocks - b)))
    return rounds


def mix(tile, items):
    total = 2 * MM_HALF
    place = [it[1] if isinstance(it, tuple) else (n + 1) * total // (len(items) + 1)
             for n, it in enumerate(items)]
    names = [it[0] if isinstance(it, tuple) else it for it in items]
    cuts = sorted(set(place + [0, MM_HALF, total]))
    events = []
    for a, b in zip(cuts, cuts[1:]):
        events += [name for name, at in zip(names, place) if at == a]
        events.append(("mm", tile, a, b))
        if b % MM_HALF == 0:
            events.append(("ev", tile, b // MM_HALF - 1))
    return events


def gla_events(hp):
    start = mix(0, [("alpha", 4), ("log1", 6), ("log2", MM_HALF)]) + ["decay", "end"]
    if hp == 0:
        return (["v0"] + start + mix(1, [("v1", 18), ("k0", 30), ("k1", 38)])
                + mix(2, [(f"kv{c}", 2 + 3 * c) for c in range(NCH - 1)])
                + mix(3, [(f"sc{r}", 2 + 3 * r) for r in range(4)] + [(f"o{r}", 18 + 8 * r) for r in range(4)])
                + ["norm"] + mix(4, [(f"out{r}", 26 + 5 * r) for r in range(4)]))
    return (start + mix(1, [("v0", 18), ("k0", 30), ("k1", 38)])
            + mix(2, [("v1", 5)] + [(f"kv{c}", 12 + 3 * c) for c in range(NCH - 4)])
            + mix(3, [(f"kv{NCH - 4 + c}", 3 * c) for c in range(3)] + [(f"sc{r}", 9 + 3 * r) for r in range(4)]
                  + [(f"o{r}", 24 + 6 * r) for r in range(4)])
            + ["norm", "gate", ("gm", 0, 24), ("gs", 0), ("gev", 0), ("gs", 1), ("gm", 24, 34), "out0", ("gs", 2),
               ("gm", 34, 38), "out1", ("gs", 3), ("gm", 38, 42), "out2", ("gm", 42, 48), ("gev", 1), "out3"])


def turn_numbers(hp):
    numbers, at = {}, 0
    for ev in gla_events(hp):
        if ev in ("v0", "v1", "k0", "k1") or isinstance(ev, str) and ev.startswith("out"):
            numbers[ev] = at
            at += 2 if ev[0] == "v" else 1
    return numbers


TURN = [turn_numbers(hp) for hp in range(2)]
ROUNDS = plan_rounds()
RPP = len(ROUNDS)
R0 = 2 * KT
LAST_ROUND = {r[2]: n for n, r in enumerate(ROUNDS) if r[0] == "w"}


def stickbreak_gla_hybrid(nc, x, g_pre, w_in, b_gate, w_alpha_up, b_alpha_up, g_gla_norm,
                          w_o_sb, w_o_gla, w_out, g_final, out):
    x_rows = x[0].rearrange("(t p) d -> t p d", p=P)
    out_rows = out[0].rearrange("(t p) d -> t p d", p=P)
    w_in_v = w_in[0].rearrange("(k p) c -> p k c", p=P)
    wo_sb_v = w_o_sb[0].rearrange("(k p) c -> p k c", p=P)
    wo_gla_v = w_o_gla[0].rearrange("(k p) c -> p k c", p=P)
    w_out_v = w_out[0].rearrange("(k p) c -> p k c", p=P)

    with ExitStack() as ctx:
        base = (nc.sbuf_base + 63) // 64 * 64
        K = 1024

        def at(name, kb, shape, dt=F32):
            return nc.alloc_sbuf_tensor_at(name, shape, dt, offset=base + int(kb * K))

        w_raw = at("w_raw", 0, [P, 2, KT, P])
        w_hi = at("w_hi", 8, [P, 2, KT, P], F32R)
        w_lo = at("w_lo", 16, [P, 2, KT, P], F32R)
        ident = at("ident", 24, [P, P])
        ident_bf = at("ident_bf", 24.5, [P, P], BF16)
        mask_neg = at("mask_neg", 24.75, [P, P], BF16)
        vec_rows = at("vec_rows", 25, [27, P])
        cols = at("cols", 25.5, [P, 27])
        scratch = at("scratch", 25.6875, [P, 1])
        stats = at("stats", 25.75, [P, 64])
        w_lr = at("w_lr", 26, [P, KT, 2 * RANK], F32R)
        w_up = at("w_up", 27, [2 * RANK, GKW])
        h_hi = at("h_hi", 28, [P, KT, SEQ], F32R)
        h_lo = at("h_lo", 60, [P, KT, SEQ], F32R)
        G = at("G", 92, [P, 8, SEQ])
        F = 124
        x_t = at("x_t", F, [P, ST, D])
        junk = at("junk", F + 32, [P, D])
        lr_raw = at("lr_raw", F + 36, [P, KT, RANK])
        wt_hi = [at("wt_hi0", 108, [P, 6, 256], F32R), at("wt_hi1", F + 8, [P, 8, 256], F32R)]
        wt_lo = [at("wt_lo0", 114, [P, 6, 256], F32R), at("wt_lo1", F + 16, [P, 8, 256], F32R)]
        stage_q = at("stage_q", F, [P, SEQ])
        stage_k = at("stage_k", F + 4, [P, SEQ])
        q_st = [at(f"q_st{e}", F + 24 + 4 * e, [P, SEQ], F32R) for e in range(2)]
        k_hi = [at(f"k_hi{e}", F + 32 + 4 * e, [P, SEQ], F32R) for e in range(2)]
        k_lo = [at(f"k_lo{e}", F + 40 + 4 * e, [P, SEQ], F32R) for e in range(2)]
        v_t = at("v_t", F + 48, [P, SEQ])
        v_st = at("v_st", F + 52, [P, 2, ST, P], F32R)
        surv = at("surv", F + 60, [P, 2, SEQ + 8])
        beta = at("beta", F + 68.125, [P, 2, SEQ])
        z_silu = at("z_silu", F + 76.25, [P, SEQ])
        z_sig = at("z_sig", 120, [P, HALF])
        o_low = at("o_low", 122, [P, 2, 256])
        reset = at("reset", F + 8, [P, SEQ])
        t12 = at("t12", F + 12, [P, 2, SEQ])
        t3 = at("t3", F + 20, [P, SEQ])
        q_dec = at("q_dec", F + 24, [P, SEQ])
        k_inv = at("k_inv", F + 28, [P, SEQ])
        k_end = at("k_end", F + 32, [P, ST, P])
        v_nat = at("v_nat", F + 36, [P, ST, 2 * DV])
        state = at("state", F + 52, [P, NCH, DV])
        sT = at("sT", F + 68, [P, 2, ST, P])
        gz = at("gz", F + 60, [P, 2, SEQ])
        gz_sig = at("gz_sig", F + 76, [P, HALF])
        mask4 = at("mask4", F + 78, [P, 4, P])
        lr_t = at("lr_t", F + 44, [2 * RANK, SEQ])
        o_nat = t12[:, :, :].rearrange("p a (b c) -> p a b c", b=ST)
        g_hi = at("g_hi", F, [P, 8, SEQ], F32R)
        g_lo = at("g_lo", F + 32, [P, 8, SEQ], F32R)
        gate = at("gate", F + 68, [P, 2, SEQ])
        gate_bias = at("gate_bias", F + 80.5, [P, 2, 2])
        y_g = [at("y_g0", F + 64, [P, 2, HALF]), at("y_g1", F + 76, [P, 2, HALF])]
        G_SLOT = [0, 1, 5, 6, 2, 3, 4, 7]
        mT = at("mT", 92, [P, KT, SEQ])
        wout_raw = at("wout_raw", 28, [P, KT, D])
        wout_hi = [at("wout_hi0", 60, [P, KT, HALF], F32R), at("wout_hi1", F, [P, KT, HALF], F32R)]
        wout_lo = [at("wout_lo0", 76, [P, KT, HALF], F32R), at("wout_lo1", F + 16, [P, KT, HALF], F32R)]
        x_res = at("x_res", F + 32, [P, 2, D])
        y_row = at("y_row", F + 40, [P, 2, D])
        y_out = at("y_out", F + 48, [P, 2, D])
        g_fin = at("g_fin", F + 56, [P, D])
        junk5 = at("junk5", F + 60, [P, D])
        g_fin_row = at("g_fin_row", F + 64, [1, D])

        def bank(name, n=1):
            return ctx.enter_context(nc.psum_tensor(name, [P, n * HALF], F32))

        pj = [bank("pj0"), bank("pj1")]
        tr = [bank("tr0"), bank("tr1")]
        sc = bank("sc", 2)
        ob = [bank("ob0"), bank("ob1")]
        tr4 = [tr[0], tr[1], ob[0], ob[1]]
        ring4 = [sc[:, 0:HALF], sc[:, HALF:2 * HALF], ob[0][:, :], ob[1][:, :]]

        def sem(name):
            return ctx.enter_context(nc.semaphore(name))

        const_done = sem("const_done")
        vec_loaded = sem("vec_loaded")
        vec_turned = sem("vec_turned")
        cols_ready = sem("cols_ready")
        x_loaded = [sem(f"x_loaded{t}") for t in range(ST)]
        sq_done = sem("sq_done")
        rstd_ready = sem("rstd_ready")
        x_normed = sem("x_normed")
        lr_loaded = sem("lr_loaded")
        lr_split = sem("lr_split")
        raw_loaded = [sem("raw_loaded0"), sem("raw_loaded1")]
        hi_done = sem("hi_done")
        lo_done = sem("lo_done")
        proj_ready = sem("proj_ready")
        proj_act = sem("proj_act")
        proj_free = sem("proj_free")
        stack_hi = sem("stack_hi")
        stack_ready = sem("stack_ready")
        scores_ready = sem("scores_ready")
        sig_done = sem("sig_done")
        scan_done = sem("scan_done")
        w_ready = sem("w_ready")
        tr_ready = sem("tr_ready")
        tr_act = sem("tr_act")
        tr_free = sem("tr_free")
        av_done = sem("av_done")
        o_copied = sem("o_copied")
        o_free = sem("o_free")
        g_done = sem("g_done")
        q4_ready = sem("q4_ready")
        q4_act = sem("q4_act")
        q4_free = sem("q4_free")
        act_step = sem("act_step")
        dve_step = sem("dve_step")
        bias_ready = sem("bias_ready")
        slot_seen = sem("slot_seen")
        gate_ready = sem("gate_ready")
        gate_free = sem("gate_free")
        y_ready = sem("y_ready")
        y_free = sem("y_free")
        m_ready = sem("m_ready")
        gs_hi = sem("gs_hi")
        gs_lo = sem("gs_lo")
        wout_loaded = [sem(f"wout_loaded{c}") for c in range(KT)]
        m0_hi = sem("m0_hi")
        m0_lo = sem("m0_lo")
        wout_h = sem("wout_h")
        wout_l = sem("wout_l")
        fin_loaded = sem("fin_loaded")
        fin_bc = sem("fin_bc")
        xr_loaded = [sem("xr_loaded0"), sem("xr_loaded1")]
        o5_ready = sem("o5_ready")
        o5_free = sem("o5_free")
        ss5 = sem("ss5")
        rstd5 = sem("rstd5")
        y_done = sem("y_done")
        stored = [sem("stored0"), sem("stored1")]

        block = ctx.enter_context(nc.Block())

        N3, N4, N5 = 19, 28, 28 + 3 * KT
        BODY = {0: [("v", 1), ("z", 0), ("z", 1), ("q", 1), ("k", 1)],
                1: [("v", 2), ("v", 3), ("z", 2), ("z", 3)]}

        def bank_no(n):
            return 2 * n + (2 if n >= N3 else 0)

        BANK_LR = 2 * N3

        def body_tile(hp, j):
            return N3 + (5 if hp else 0) + j

        def body_col(kind, n):
            return {"v": COL_GV, "z": COL_GZ, "q": COL_GQ, "k": COL_GK}[kind] + P * n

        R3 = R0 + RPP * PAIRS
        R_BODY = 10
        Q_BODY = 2 + (NCH - 1) + 4 + 4

        def load_small(sp):
            sp.dma_start(vec_rows[0:8, :], g_pre[0].rearrange("(a p) -> a p", p=P)).then_inc(vec_loaded, 16)
            sp.dma_start(vec_rows[8:24, :], b_gate[0].rearrange("(a p) -> a p", p=P)).then_inc(vec_loaded, 16)
            sp.dma_start(vec_rows[24:26, :], b_alpha_up[0].rearrange("(a p) -> a p", p=P))\
                .then_inc(vec_loaded, 16)
            sp.dma_start(vec_rows[26:27, :], g_gla_norm).then_inc(vec_loaded, 16)
            for c in range(2):
                sp.dma_start(w_up[RANK * c:RANK * (c + 1), :], w_alpha_up[0]).then_inc(vec_loaded, 16)

        @block.sync
        def _(sp):
            def load_x(tiles):
                for t in tiles:
                    sp.dma_start(x_t[:, t, :], x_rows[t]).then_inc(x_loaded[t], 16)

            def load(n, col, slot):
                if not isinstance(n, int):
                    col = sp.snap(col)
                if not isinstance(n, int) or n >= 2:
                    sp.wait_ge(lo_done, n - 1)
                sp.dma_start(w_raw[:, slot, :, :], w_in_v[:, :, bass.ds(col, P)])\
                    .then_inc(raw_loaded[slot], 16)

            load_x(range(4))
            load_small(sp)
            load(0, COL_Q, 0)
            load(1, COL_K, 1)
            load_x(range(4, 8))
            sp.dma_start(lr_raw[:, :, :], w_in_v[:, :, COL_LR:COL_LR + RANK]).then_inc(lr_loaded, 16)
            load(2, COL_V, 0)
            with sp.Fori(0, PAIRS - 1) as i:
                load(4 * i + 3, COL_Z + P * i, 1)
                load(4 * i + 4, COL_Q + P + P * i, 0)
                load(4 * i + 5, COL_K + P + P * i, 1)
                load(4 * i + 6, COL_V + P + P * i, 0)
            load(15, COL_Z + P * (PAIRS - 1), 1)
            load(16, COL_GQ, 0)
            load(17, COL_GK, 1)
            load(18, COL_GV, 0)
            for hp in range(2):
                for j, (kind, m) in enumerate(BODY[hp]):
                    load(body_tile(hp, j), body_col(kind, m), body_tile(hp, j) % 2)
            with sp.Fori(0, KT // 2) as jj:
                for u in range(2):
                    n = 6 * jj + N4 + 3 * u
                    load(n, jj * (2 * P) + COL_GA + P * u, (N4 + 3 * u) % 2)
                    load(n + 1, jj * (2 * P) + COL_GB + P * u, (N4 + 3 * u + 1) % 2)
                    slot = (N4 + 3 * u + 2) % 2
                    c = jj * (2 * P) + P * u
                    sp.wait_ge(lo_done, n + 1)
                    sp.sem_inc(slot_seen, 1)
                    sp.dma_start(w_raw[:, slot, 0:4, :], wo_sb_v[:, :, bass.ds(c, P)])\
                        .then_inc(raw_loaded[slot], 16)
                    sp.dma_start(w_raw[:, slot, 4:8, :], wo_gla_v[:, :, bass.ds(c, P)])\
                        .then_inc(lr_loaded, 16)
            sp.wait_ge(gate_ready, 4 * KT)
            for c in range(KT):
                e, kk = c // 4, 2 * (c % 4)
                sp.dma_start(wout_raw[:, kk:kk + 2, e * HALF:(e + 1) * HALF],
                             w_out_v[:, kk:kk + 2, e * HALF:(e + 1) * HALF]).then_inc(wout_loaded[c], 16)
            def store(t):
                for e in range(2):
                    es = slice(HALF * e, HALF * e + HALF)
                    sp.wait_ge(y_done, 2 * t + e + 1)
                    sp.dma_start(out_rows[t][:, es], y_out[:, t % 2, es]).then_inc(stored[t % 2], 16)

            sp.wait_ge(m_ready, 2 * KT)
            sp.dma_start(g_fin_row[0:1, :], g_final.rearrange("(a d) -> a d", a=1)).then_inc(fin_loaded, 16)
            for t in range(ST):
                if t >= 2:
                    sp.wait_ge(o5_free, 2 * (t - 2) + 2)
                sp.dma_start(x_res[:, t % 2, :], x_rows[t]).then_inc(xr_loaded[t % 2], 16)
                if t >= 1:
                    store(t - 1)
            store(ST - 1)
            for s in stored:
                sp.wait_ge(s, 16 * ST)

        @block.gpsimd
        def _(pool):
            pool.memset(ident[:, :], 0.0).then_inc(const_done, 1)
            pool.memset(ident_bf[:, :], 0.0).then_inc(const_done, 1)
            pool.memset(mask_neg[:, :], 0.0).then_inc(const_done, 1)
            pool.wait_ge(const_done, 3)
            for m in (ident, ident_bf):
                pool.affine_select(out=m[:, :], in_=m[:, :], compare_op=ALU.not_equal, fill=1.0, base=0,
                                   pattern=[[-1, P]], channel_multiplier=1).then_inc(const_done, 1)
            pool.affine_select(out=mask_neg[:, :], in_=mask_neg[:, :], compare_op=ALU.is_gt, fill=NEG,
                               base=0, pattern=[[-1, P]], channel_multiplier=1).then_inc(const_done, 1)
            pool.wait_ge(g_done, 8 * PAIRS)
            pool.memset(mask4[:, :, :], 1.0).then_inc(const_done, 1)
            pool.memset(reset[:, :], 1.0).then_inc(const_done, 1)
            pool.memset(sT[:, :, :, :], 0.0).then_inc(const_done, 1)
            pool.memset(state[:, 0, :], 0.0).then_inc(const_done, 1)
            pool.wait_ge(const_done, 10)
            pool.affine_select(out=mask4[:, :, :], in_=mask4[:, :, :], compare_op=ALU.is_ge, fill=0.0, base=0,
                               pattern=[[0, 4], [1, P]], channel_multiplier=-1).then_inc(const_done, 1)
            pool.wait_ge(const_done, 11)
            pool.memset(mask4[0:CH, :, CH:P], 0.0).then_inc(const_done, 1)
            pool.memset(reset[:, 0:SEQ:CH], 0.0).then_inc(const_done, 1)
            pool.wait_ge(fin_loaded, 16)
            pool.partition_broadcast(g_fin[:, :], g_fin_row[0:1, :], P).then_inc(fin_bc, 1)

        @block.tensor
        def _(pe):
            pe.sem_inc(y_ready, 1)
            pe.wait_ge(const_done, 6)
            pe.wait_ge(vec_loaded, 96)
            pe.transpose(sc[:, 0:27], vec_rows[:, :], ident[0:27, 0:27]).then_inc(vec_turned, 1)

            def turn_x(rounds):
                for r in rounds:
                    g, k = r // KT, r % KT
                    if r >= 4:
                        pe.wait_ge(tr_free, r - 3)
                    for t in range(4):
                        if k == 0:
                            pe.wait_ge(x_normed, 4 * g + t + 1)
                        mm = pe.transpose(tr4[r % 4][:, P * t:P * t + P],
                                          x_t[:, 4 * g + t, P * k:P * k + P], ident[:, :])
                    mm.then_inc(tr_ready, 1)

            def projection(n, slot, c, bank, h_k_p):
                h, k, p = h_k_p
                if h == 0 and k == 0 and p == 0:
                    pe.wait_ge(lo_done, n + 1)
                if p == 0 and isinstance(c, int) and c in (0, 2):
                    pe.wait_ge(tr_free, KT * h + k + 1)
                if k == 0 and p == 0 and not (isinstance(c, int) and c < 2):
                    pe.wait_ge(proj_free, c - 1)
                mm = pe.matmul(pj[bank][:, :], (w_lo if p == 2 else w_hi)[:, slot, k, :],
                               (h_lo if p == 1 else h_hi)[:, k, HALF * h:HALF * h + HALF],
                               start=(k == 0 and p == 0), stop=(k == KT - 1 and p == 2))
                if k == KT - 1 and p == 2:
                    mm.then_inc(proj_ready, 1)

            def half_tile(n, c, h):
                for k in range(KT):
                    for p in range(3):
                        projection(n, n % 2, c, c % 2, (h, k, p))

            turn_x(range(4))
            for k in range(KT):
                if k < 4:
                    turn_x([4 + k])
                for p in range(3):
                    projection(0, 0, 0, 0, (0, k, p))
            for m in range(MM_HALF):
                turn_x([KT + r for r in range(KT) if m == 13 + 11 * r // KT])
                projection(1, 1, 1, 1, (0, m // 3, m % 3))
            half_tile(0, 2, 1)
            half_tile(1, 3, 1)
            half_tile(2, 4, 0)
            half_tile(2, 5, 1)

            def pair(i):
                plan = plan_projection()
                for step in range(STEPS):
                    if step < 16:
                        e, qt = step // 8, step % 8
                        if qt == 0:
                            pe.wait_ge(stack_ready, 6 * i + 3 * e + 3)
                        pe.wait_ge(sig_done, 16 * i + step + 1)
                        keys = (qt + 1) * P
                        for c0 in range(0, keys, HALF):
                            c1 = min(keys, c0 + HALF)
                            last = c1 == keys
                            lhs = q_st[e][:, P * qt:P * qt + P]
                            pe.matmul(sc[:, c0:c1], lhs, k_hi[e][:, c0:c1], start=True, stop=False)
                            mm = pe.matmul(sc[:, c0:c1], lhs, k_lo[e][:, c0:c1], start=False, stop=not last)
                        mm = pe.matmul(sc[:, keys - P:keys], ident_bf[:, :], mask_neg[:, :],
                                       start=False, stop=True)
                        mm.then_inc(scores_ready, 1)
                    for n, r in enumerate(ROUNDS):
                        if r[0] == "v" and r[1] == step:
                            pe.wait_ge(proj_free, 8 * i + 6)
                            pe.wait_ge(tr_free, RPP * i + R0 + n - 1)
                            for b in range(4):
                                mm = pe.transpose(tr[n % 2][:, P * b:P * b + P],
                                                  v_t[:, P * (4 * r[2] + b):P * (4 * r[2] + b) + P], ident[:, :])
                            mm.then_inc(tr_ready, 1)
                    for j, h, k, p in plan[step]:
                        projection(4 * i + 3 + j, (3 + j) % 2, 8 * i + 6 + 2 * j + h, h, (h, k, p))
                    if step >= 3 and step % 2:
                        gg = (step - 3) // 2
                        e, g = gg // 4, gg % 4
                        pe.wait_ge(tr_free, RPP * i + R0 + LAST_ROUND[2 * gg + 1] + 1)
                        pe.wait_ge(o_free, 8 * i + gg + 1)
                        blocks = 2 * g + 2
                        for b in range(blocks):
                            c0 = P * max(0, b - 2 * g)
                            for part in (wt_hi, wt_lo):
                                mm = pe.matmul(ob[gg % 2][:, c0:256], v_st[:, e, b, :], part[g % 2][:, b, c0:256],
                                               start=(b == 0 and part is wt_hi),
                                               stop=(b == blocks - 1 and part is wt_lo))
                        mm.then_inc(av_done, 1)
                    for n, r in enumerate(ROUNDS):
                        if r[0] == "w" and r[1] == step:
                            unit, b0, nb = r[2:]
                            pe.wait_ge(w_ready, 16 * i + unit + 1)
                            pe.wait_ge(tr_free, RPP * i + R0 + n - 1)
                            for b in range(nb):
                                mm = pe.transpose(tr[n % 2][:, P * b:P * b + P],
                                                  beta[:, unit % 2, P * (b0 + b):P * (b0 + b) + P], ident[:, :])
                            mm.then_inc(tr_ready, 1)

            with pe.Fori(0, PAIRS - 1) as i:
                pair(i)
            pair(PAIRS - 1)

            for h in range(2):
                pe.wait_ge(proj_free, BANK_LR + h - 1)
                for k in range(KT):
                    for part in (h_hi, h_lo):
                        mm = pe.matmul(pj[h][0:2 * RANK, :], w_lr[:, k, :], part[:, k, HALF * h:HALF * h + HALF],
                                       start=(k == 0 and part is h_hi), stop=(k == KT - 1 and part is h_lo))
                mm.then_inc(proj_ready, 1)

            def turn(n, src, first):
                pe.wait_ge(tr_free, n - 1)
                for b in range(4):
                    mm = pe.transpose(tr[n % 2][:, P * b:P * b + P], src[:, P * (first + b):P * (first + b) + P],
                                      ident[:, :])
                mm.then_inc(tr_ready, 1)

            def gate_product(slot, c0, m):
                h, k, p = m // MM_HALF, m % MM_HALF // 3, m % 3
                if k == 0 and p == 0:
                    pe.wait_ge(gate_free, c0 + h + 1)
                mm = pe.matmul(pj[h][:, :], (w_lo if p == 2 else w_hi)[:, slot, k, :],
                               (h_lo if p == 1 else h_hi)[:, k, HALF * h:HALF * h + HALF],
                               start=(k == 0 and p == 0), stop=(k == KT - 1 and p == 2))
                if k == KT - 1 and p == 2:
                    mm.then_inc(gate_ready, 1)

            def gate_tile(n, slot, c0):
                pe.wait_ge(lo_done, n + 1)
                for m in range(2 * MM_HALF):
                    gate_product(slot, c0, m)

            for hp in range(2):
                q0, r0 = Q_BODY * hp, R3 + R_BODY * hp
                for ev in gla_events(hp):
                    kind = ev if isinstance(ev, str) else ev[0]
                    if kind == "alpha":
                        for h in range(2):
                            q = q0 + h
                            pe.wait_ge(proj_free, BANK_LR + 2)
                            if q >= 4:
                                pe.wait_ge(q4_free, q - 3)
                            else:
                                pe.wait_ge(o_free, 2 + 8 * PAIRS)
                            pe.matmul(ring4[q % 4], w_up[:, P * hp:P * hp + P],
                                      lr_t[:, HALF * h:HALF * h + HALF], start=True, stop=True).then_inc(q4_ready, 1)
                    elif kind == "mm":
                        n = body_tile(hp, ev[1])
                        for m in range(ev[2], ev[3]):
                            h = m // MM_HALF
                            projection(n, n % 2, bank_no(n) + h, h, (h, m % MM_HALF // 3, m % 3))
                    elif kind in ("v0", "v1"):
                        j = int(kind[1])
                        n = 18 + j if hp == 0 else body_tile(1, j)
                        pe.wait_ge(proj_free, bank_no(n) + 2)
                        for r in range(2):
                            turn(r0 + TURN[hp][kind] + r, v_t[:, :], 4 * r)
                    elif kind in ("k0", "k1"):
                        r = int(kind[1])
                        pe.wait_ge(dve_step, 7 * hp + 7)
                        turn(r0 + TURN[hp][kind], t3[:, :], 4 * r)
                    elif kind.startswith("kv"):
                        c = int(kind[2:])
                        q, row, b = q0 + 2 + c, CH * (c % 2), c // 2
                        if c == 0:
                            pe.wait_ge(tr_free, r0 + 6)
                        if q >= 4:
                            pe.wait_ge(q4_free, q - 3)
                        pe.matmul(ring4[q % 4][:, 0:2 * DV], k_end[row:row + CH, b, :], v_nat[row:row + CH, b, :],
                                  start=True, stop=True).then_inc(q4_ready, 1)
                    elif kind.startswith("sc"):
                        r = int(kind[2:])
                        q, e, b0 = q0 + 2 + NCH - 1 + r, r % 2, 4 * (r // 2)
                        pe.wait_ge(q4_free, q - 3)
                        for b in range(b0, b0 + 4):
                            mm = pe.matmul(ring4[q % 4][:, P * (b - b0):P * (b - b0) + P],
                                           k_inv[HD * e:HD * e + HD, P * b:P * b + P],
                                           q_dec[HD * e:HD * e + HD, P * b:P * b + P], start=True, stop=True)
                        mm.then_inc(q4_ready, 1)
                    elif kind in ("o0", "o1", "o2", "o3"):
                        r = int(kind[1])
                        q, e, b0 = q0 + 2 + NCH - 1 + 4 + r, r % 2, 4 * (r // 2)
                        pe.wait_ge(q4_free, q0 + 2 + NCH - 1 + r + 1)
                        for b in range(b0, b0 + 4):
                            o = ring4[q % 4][:, P * (b - b0):P * (b - b0) + P]
                            pe.matmul(o, sT[:, e, b, :], v_nat[:, b, DV * e:DV * e + DV], start=True, stop=False,
                                      skip_group_check=True)
                            for cc in range(2):
                                s0 = P * b + CH * cc
                                mm = pe.matmul(o[CH * cc:CH * cc + CH, :], q_dec[HD * e:HD * e + HD, s0:s0 + CH],
                                               state[HD * e:HD * e + HD, 2 * b + cc, :], start=False,
                                               stop=(cc == 1), skip_group_check=True)
                        mm.then_inc(q4_ready, 1)
                    elif kind == "gm":
                        for m in range(ev[1], ev[2]):
                            if m == 0:
                                pe.wait_ge(lo_done, N4 + 1)
                            if m % MM_HALF == 0:
                                pe.wait_ge(proj_free, bank_no(N4) - 1 + m // MM_HALF)
                            gate_product(N4 % 2, 0, m)
                    elif kind.startswith("out"):
                        r = int(kind[3])
                        pe.wait_ge(rstd_ready, ST + 2 * hp + 2)
                        turn(r0 + 6 + r, o_nat[:, r // 2, :, :].rearrange("p b q -> p (b q)"), 4 * (r % 2))

            pe.wait_ge(q4_free, 2 * Q_BODY)

            def merge(jj, last):
                for u in range(2):
                    n = 6 * jj + N4 + 3 * u
                    c0 = 8 * jj + 4 * u
                    gate_tile(n + 1, (N4 + 3 * u + 1) % 2, c0 + 2)
                    slot = (N4 + 3 * u + 2) % 2
                    pe.wait_ge(lo_done, n + 3)
                    for h in range(2):
                        for br in range(2):
                            pe.wait_ge(gs_lo, 4 * br + 4)
                            pe.wait_ge(y_free, c0 + 2 * h + br + 1)
                            for k in range(4 * br, 4 * br + 4):
                                for p in range(3):
                                    mm = pe.matmul(ring4[2 * h + br], (w_lo if p == 2 else w_hi)[:, slot, k, :],
                                                   (g_lo if p == 1 else g_hi)[:, G_SLOT[k], HALF * h:HALF * h + HALF],
                                                   start=(k == 4 * br and p == 0), stop=(k == 4 * br + 3 and p == 2))
                            mm.then_inc(y_ready, 1)
                    if not (last and u == 1):
                        gate_tile(n + 3, (N4 + 3 * u + 3) % 2, c0 + 4)

            with pe.Fori(0, KT // 2 - 1) as jj:
                merge(jj, False)
            merge(KT // 2 - 1, True)

            for t in range(ST):
                slot = (N5 + t) % 2
                if t:
                    pe.wait_ge(lo_done, N5 + t)
                for e in range(2):
                    c = 2 * t + e
                    if c >= 4:
                        pe.wait_ge(o5_free, c - 3)
                    else:
                        pe.wait_ge(y_free, 4 * KT + c + 1)
                    for k in range(KT):
                        if t == 0 and k % 2 == 0:
                            pe.wait_ge(wout_l, 4 * e + k // 2 + 1)
                        if c == 0 and k in (0, KT - 1):
                            pe.wait_ge(m0_lo, 2 if k else 1)
                        for p in range(3):
                            mm = pe.matmul(ring4[c % 4], (w_lo if p == 2 else w_hi)[:, slot, k, :],
                                           (wout_lo if p == 1 else wout_hi)[e][:, k, :],
                                           start=(k == 0 and p == 0), stop=(k == KT - 1 and p == 2))
                    mm.then_inc(o5_ready, 1)

        @block.scalar
        def _(act):
            act.sem_inc(sig_done, 1)
            act.sem_inc(gate_free, 2)
            act.wait_ge(const_done, 1)
            act.wait_ge(cols_ready, 1)
            act.activation(scratch[:, :], stats[:, 63:64], ACT.Sqrt)

            def row_norms(tiles):
                for t in tiles:
                    act.wait_ge(x_loaded[t], 16)
                    if t:
                        act.wait_ge(sq_done, 2 * t)
                    act.activation(junk[:, :], x_t[:, t, :], ACT.Square, accum_out=stats[:, t:t + 1])\
                        .then_inc(sq_done, 1)
                    act.wait_ge(sq_done, 2 * t + 1)
                    act.activation(stats[:, 8 + t:9 + t], stats[:, t:t + 1], ACT.Sqrt,
                                   bias=stats[:, 63:64], scale=1.0 / D).then_inc(sq_done, 1)

            def h_high(rounds):
                for r in rounds:
                    g, k = r // KT, r % KT
                    act.wait_ge(tr_ready, r + 1)
                    act.activation(h_hi[:, k, HALF * g:HALF * g + HALF], tr4[r % 4][:, :], ACT.Copy,
                                   scale=cols[:, k:k + 1]).then_inc(tr_act, 1)

            def high_part(n, slot, loads, done_sem, done):
                act.wait_ge(raw_loaded[slot], 16 * loads)
                if done is not None:
                    act.wait_ge(done_sem, done)
                act.activation(w_hi[:, slot, :, :], w_raw[:, slot, :, :], ACT.Copy).then_inc(hi_done, 1)

            def stage(dst, c, h, bank):
                act.wait_ge(proj_ready, c + 1)
                act.activation(dst[:, HALF * h:HALF * h + 256], pj[bank][:, 0:256], ACT.Copy).then_inc(proj_act, 1)

            def stack(e, part):
                own, other = slice(HD * e, HD * e + HD), slice(HD * (1 - e), HD * (1 - e) + HD)
                if part == 0:
                    act.activation(q_st[e][own, :], stage_q[own, :], ACT.Copy).then_inc(stack_hi, 1)
                else:
                    act.activation(k_hi[e][own if part == 1 else other, :], stage_k[own, :], ACT.Copy)\
                        .then_inc(stack_hi, 1)

            row_norms(range(4))
            high_part(0, 0, 1, None, None)
            high_part(1, 1, 1, None, None)
            act.wait_ge(cols_ready, 3)
            h_high(range(4))
            row_norms([4])
            h_high(range(4, KT))
            row_norms(range(5, ST))
            stage(stage_q, 0, 0, 0)
            h_high(range(KT, R0))
            stage(stage_k, 1, 0, 1)
            stage(stage_q, 2, 1, 0)
            high_part(2, 0, 2, proj_ready, 3)
            stage(stage_k, 3, 1, 1)
            act.wait_ge(proj_free, 4)
            for part in range(3):
                stack(0, part)
            stage(v_t, 4, 0, 0)
            high_part(3, 1, 2, proj_ready, 4)
            stage(v_t, 5, 1, 1)
            act.wait_ge(lr_loaded, 16)
            act.activation(w_lr[:, :, 0:RANK], lr_raw[:, :, :], ACT.Copy).then_inc(lr_split, 1)
            act.wait_ge(lr_split, 2)

            def pair(i, last):
                plan = plan_projection()
                dsts = [None, stage_q, stage_k, v_t]
                act.activation(scratch[:, :], stats[:, 63:64], ACT.Sigmoid)
                for step in range(STEPS):
                    if step < 16:
                        keys = (step % 8 + 1) * P
                        act.wait_ge(scores_ready, 16 * i + step + 1)
                        act.activation(surv[:, step % 2, 0:keys], sc[:, 0:keys], ACT.Sigmoid, scale=-HD ** -0.5)
                        act.activation(beta[:, step % 2, 0:keys], sc[:, 0:keys], ACT.Sigmoid, scale=HD ** -0.5)\
                            .then_inc(sig_done, 1)
                    for n, r in enumerate(ROUNDS):
                        if r[0] == "v" and r[1] == step:
                            act.wait_ge(tr_ready, RPP * i + R0 + n + 1)
                            act.activation(v_st[:, :, 4 * r[2]:4 * r[2] + 4, 0:HD],
                                           tr[n % 2][:, :].rearrange("p (b e d) -> p e b d", d=HD, e=2),
                                           ACT.Copy).then_inc(tr_act, 1)
                    if step in SECOND_STEPS:
                        stack(1, SECOND_STEPS.index(step))
                    if step in STACK_STEPS and not last:
                        part = STACK_STEPS.index(step)
                        act.wait_ge(proj_free, 8 * i + (12 if part else 10))
                        stack(0, part)
                    for j, h, k, p in plan[step]:
                        if k < KT - 1 or p < 2:
                            continue
                        c = 8 * i + 6 + 2 * j + h
                        if h == 0:
                            high_part(None, j % 2, 2 * i + 3 + j // 2, proj_ready, 8 * i + 6 + 2 * j)
                        if j == 0:
                            act.wait_ge(proj_ready, c + 1)
                            if h == 1:
                                act.wait_ge(proj_free, c)
                            act.activation(z_sig[:, :], pj[h][:, :], ACT.Sigmoid).then_inc(proj_act, 1)
                        else:
                            act.wait_ge(stack_ready, 6 * i + 6)
                            stage(dsts[j], c, h, h)
                    if step >= 3 and step % 2:
                        gg = (step - 3) // 2
                        e = gg // 4
                        act.wait_ge(av_done, 8 * i + gg + 1)
                        act.activation(o_low[HD * e:HD * e + HD, gg % 2, :], ob[gg % 2][HD:P, 0:256],
                                       ACT.Copy).then_inc(o_copied, 1)
                    for n, r in enumerate(ROUNDS):
                        if r[0] == "w" and r[1] == step:
                            unit, b0, nb = r[2:]
                            g = unit % 8 // 2
                            act.wait_ge(tr_ready, RPP * i + R0 + n + 1)
                            act.activation(wt_hi[g % 2][:, b0:b0 + nb, P * (unit % 2):P * (unit % 2) + P],
                                           tr[n % 2][:, 0:P * nb].rearrange("p (b q) -> p b q", q=P),
                                           ACT.Copy).then_inc(tr_act, 1)

            with act.Fori(0, PAIRS - 1) as i:
                pair(i, False)
            pair(PAIRS - 1, True)

            act.wait_ge(o_free, 2 + 8 * PAIRS)
            act.wait_ge(g_done, 8 * PAIRS)
            for h in range(2):
                act.wait_ge(proj_ready, BANK_LR + h + 1)
                act.activation(lr_t[:, HALF * h:HALF * h + 256], pj[h][0:2 * RANK, 0:256], ACT.Copy)\
                    .then_inc(proj_act, 1)

            def gz_sigmoid(c, h):
                act.wait_ge(proj_ready, c + 1)
                act.wait_ge(proj_free, c)
                act.activation(gz_sig[:, :], pj[h][:, :], ACT.Sigmoid).then_inc(proj_act, 1)

            def body_evacuate(hp, j, h):
                n = body_tile(hp, j)
                kind, m = BODY[hp][j]
                c = bank_no(n) + h
                if kind == "z":
                    gz_sigmoid(c, h)
                elif kind == "v":
                    stage(v_t, c, h, h)
                else:
                    act.wait_ge(dve_step, 7 * hp + 7)
                    stage(stage_q if kind == "q" else stage_k, c, h, h)
                if h == 0:
                    m1 = n + 1
                    high_part(m1, m1 % 2, m1 // 2 + 1, proj_ready, bank_no(m1 - 2) + 2)

            def copy_round(n, dst):
                act.wait_ge(tr_ready, n + 1)
                act.activation(dst, tr[n % 2][:, 0:256].rearrange("p (b d) -> p b d", d=P), ACT.Copy)\
                    .then_inc(tr_act, 1)

            def split_g(k):
                act.activation(g_hi[:, G_SLOT[k], :], G[:, k, :], ACT.Copy).then_inc(gs_hi, 1)

            def gate_half(g, h, jj, off):
                c = 8 * jj + 4 * off + 2 * g + h
                act.wait_ge(gate_ready, c + 1)
                act.activation(gate[:, g, HALF * h:HALF * h + HALF], pj[h][:, :], ACT.Sigmoid,
                               bias=gate_bias[:, off % 2, g:g + 1]).then_inc(gate_free, 1)

            def gate_a_ahead(jj, off):
                for g in range(2):
                    act.activation(gate_bias[:, off % 2, g:g + 1], cols[:, bass.ds(2 * jj + 8 + 8 * g + off, 1)],
                                   ACT.Copy).then_inc(bias_ready, 1)
                act.wait_ge(bias_ready, 4 * jj + 2 * off + 2)
                high_part(None, (N4 + 3 * off + 1) % 2, 3 * jj + (N4 + 3 * off + 1) // 2 + 1, y_ready,
                          8 * jj + 4 * off + 1)
                act.wait_ge(y_free, 8 * jj + 4 * off + 4)

            t1, t2 = t12[:, 0, :], t12[:, 1, :]
            for hp in range(2):
                q0, s0, d0, r0 = Q_BODY * hp, 5 * hp, 7 * hp, R3 + R_BODY * hp
                bias = cols[:, 24 + hp:25 + hp]
                for ev in gla_events(hp):
                    kind = ev if isinstance(ev, str) else ev[0]
                    if kind == "alpha":
                        if hp:
                            act.wait_ge(tr_ready, r0)
                        for h in range(2):
                            act.wait_ge(q4_ready, q0 + h + 1)
                            act.activation(t1[:, HALF * h:HALF * h + HALF], ring4[(q0 + h) % 4], ACT.Abs,
                                           bias=bias).then_inc(q4_act, 1)
                    elif kind == "log1":
                        act.wait_ge(q4_act, (2 + 4) * hp + 2)
                        act.activation(t1, t1, ACT.Exp, scale=-1.0).then_inc(act_step, 1)
                        act.wait_ge(act_step, s0 + 1)
                        act.activation(t1, t1, ACT.Ln, bias=1.0).then_inc(act_step, 1)
                    elif kind == "log2":
                        act.wait_ge(dve_step, d0 + 2)
                        act.activation(t2, t1, ACT.Exp, scale=1.0 / 16).then_inc(act_step, 1)
                        act.activation(t3[:, :], t1, ACT.Exp, scale=-1.0 / 16).then_inc(act_step, 1)
                    elif kind == "decay":
                        act.wait_ge(dve_step, d0 + 6)
                        act.activation(t2, t2, ACT.Exp, scale=1.0 / 16).then_inc(act_step, 1)
                    elif kind == "ev":
                        body_evacuate(hp, ev[1], ev[2])
                    elif kind in ("v0", "v1"):
                        j = int(kind[1])
                        for r in range(2):
                            copy_round(r0 + TURN[hp][kind] + r, v_nat[:, 4 * r:4 * r + 2, DV * j:DV * j + DV])
                    elif kind in ("k0", "k1"):
                        r = int(kind[1])
                        copy_round(r0 + TURN[hp][kind], k_end[:, 4 * r:4 * r + 2, :])
                    elif kind in ("o0", "o1", "o2", "o3"):
                        r = int(kind[1])
                        q, e, b0 = q0 + 2 + NCH - 1 + 4 + r, r % 2, 4 * (r // 2)
                        act.wait_ge(q4_ready, q + 1)
                        if r >= 2:
                            act.wait_ge(q4_act, 6 * hp + 2 + r - 1)
                        for b in range(4):
                            sq = P * (4 * (r % 2) + b)
                            a = act.activation(t3[:, sq:sq + P], ring4[q % 4][:, P * b:P * b + P], ACT.Square,
                                               accum_out=stats[:, 16 + 8 * e + b0 + b:17 + 8 * e + b0 + b])
                        a.then_inc(q4_act, 1)
                    elif kind == "norm":
                        act.wait_ge(q4_act, 6 * hp + 6)
                        act.activation(stats[:, 32:48], stats[:, 16:32], ACT.Sqrt, bias=stats[:, 63:64],
                                       scale=1.0 / DV).then_inc(sq_done, 1)
                    elif kind == "gate":
                        gate_a_ahead(0, 0)
                    elif kind == "gev":
                        gate_half(0, ev[1], 0, 0)
                    elif kind == "gs":
                        split_g(ev[1])

            act.wait_ge(tr_free, R3 + 2 * R_BODY)
            for k in range(4, 8):
                split_g(k)

            def merge(jj, last):
                for u in range(2):
                    gate_half(1, 0, jj, u)
                    act.wait_ge(lr_loaded, 32 * jj + 16 * u + 32)
                    high_part(None, (N4 + 3 * u + 2) % 2, 3 * jj + (N4 + 3 * u + 2) // 2 + 1, gate_ready,
                              8 * jj + 4 * u + 2)
                    gate_half(1, 1, jj, u)
                    if not (last and u == 1):
                        high_part(None, (N4 + 3 * u + 3) % 2, 3 * jj + (N4 + 3 * u + 3) // 2 + 1, gate_ready,
                                  8 * jj + 4 * u + 4)
                        gate_a_ahead(jj, u + 1)
                        for h in range(2):
                            gate_half(0, h, jj, u + 1)

            with act.Fori(0, KT // 2 - 1) as jj:
                merge(jj, False)
            merge(KT // 2 - 1, True)

            def split_m(t):
                slot = (N5 + t) % 2
                if t >= 2:
                    act.wait_ge(o5_ready, 2 * (t - 2) + 2)
                act.activation(w_hi[:, slot, :, :], mT[:, :, P * t:P * t + P], ACT.Copy).then_inc(hi_done, 1)

            def split_m0(part):
                ks = slice(0, KT - 1) if part == 0 else slice(KT - 1, KT)
                act.wait_ge(m_ready, 2 * KT - 2 + 2 * part)
                act.activation(w_hi[:, N5 % 2, ks, :], mT[:, ks, 0:P], ACT.Copy).then_inc(m0_hi, 1)

            split_m0(0)
            for c in range(KT):
                e, kk = c // 4, 2 * (c % 4)
                if c == 4:
                    split_m0(1)
                    act.wait_ge(y_ready, 1 + 4 * KT)
                act.wait_ge(wout_loaded[c], 16)
                act.activation(wout_hi[e][:, kk:kk + 2, :], wout_raw[:, kk:kk + 2, HALF * e:HALF * e + HALF],
                               ACT.Copy).then_inc(wout_h, 1)
            for t in range(ST):
                if t + 1 < ST:
                    split_m(t + 1)
                act.wait_ge(o5_free, 2 * t + 2)
                act.activation(junk5[:, :], y_row[:, t % 2, :], ACT.Square, accum_out=stats[:, 48 + t % 2:49 + t % 2])\
                    .then_inc(ss5, 1)
                act.wait_ge(ss5, 2 * t + 1)
                act.activation(stats[:, 50 + t % 2:51 + t % 2], stats[:, 48 + t % 2:49 + t % 2], ACT.Sqrt,
                               bias=stats[:, 63:64], scale=1.0 / D).then_inc(ss5, 1)

        @block.vector
        def _(dve):
            dve.sem_inc(o_free, 2)
            dve.sem_inc(y_free, 4)
            dve.memset(stats[:, 63:64], EPS).then_inc(cols_ready, 1)
            dve.memset(surv[:, :, :], 1.0).then_inc(cols_ready, 1)
            def norm_rows(tiles):
                for t in tiles:
                    dve.wait_ge(sq_done, 2 * t + 2)
                    dve.reciprocal(stats[:, 8 + t:9 + t], stats[:, 8 + t:9 + t]).then_inc(rstd_ready, 1)
                    dve.wait_ge(rstd_ready, t + 1)
                    dve.tensor_scalar(x_t[:, t, :], x_t[:, t, :], stats[:, 8 + t:9 + t], None, ALU.mult)\
                        .then_inc(x_normed, 1)

            def low_part(n, slot):
                dve.wait_ge(hi_done, n + 1)
                dve.tensor_tensor(w_lo[:, slot, :, :], w_raw[:, slot, :, :], w_hi[:, slot, :, :].bitcast(F32),
                                  ALU.subtract).then_inc(lo_done, 1)

            def h_low(rounds):
                for r in rounds:
                    g, k = r // KT, r % KT
                    hs = slice(HALF * g, HALF * g + HALF)
                    dve.wait_ge(tr_act, r + 1)
                    dve.scalar_tensor_tensor(out=h_lo[:, k, hs], in0=tr4[r % 4][:, :], scalar=cols[:, k:k + 1],
                                             in1=h_hi[:, k, hs].bitcast(F32), op0=ALU.mult, op1=ALU.subtract)\
                        .then_inc(tr_free, 1)

            def stage(dst, c, h, bank):
                dve.wait_ge(proj_act, c + 1)
                dve.tensor_copy(dst[:, HALF * h + 256:HALF * h + HALF], pj[bank][:, 256:HALF]).then_inc(proj_free, 1)

            def stack(e, part, done):
                own, other = slice(HD * e, HD * e + HD), slice(HD * (1 - e), HD * (1 - e) + HD)
                dve.wait_ge(stack_hi, done + 1)
                if part == 0:
                    dve.tensor_tensor(q_st[e][other, :], stage_q[own, :], q_st[e][own, :].bitcast(F32),
                                      ALU.subtract).then_inc(stack_ready, 1)
                else:
                    dve.tensor_tensor(k_lo[e][own if part == 1 else other, :], stage_k[own, :],
                                      k_hi[e][own, :].bitcast(F32), ALU.subtract).then_inc(stack_ready, 1)

            norm_rows(range(4))
            dve.wait_ge(vec_turned, 1)
            dve.tensor_copy(cols[:, :], sc[:, 0:27]).then_inc(cols_ready, 1)
            dve.wait_ge(cols_ready, 3)
            low_part(0, 0)
            h_low(range(KT))
            low_part(1, 1)
            norm_rows(range(4, ST))
            stage(stage_q, 0, 0, 0)
            h_low(range(KT, R0))
            stage(stage_k, 1, 0, 1)
            stage(stage_q, 2, 1, 0)
            low_part(2, 0)
            stage(stage_k, 3, 1, 1)
            for part in range(3):
                stack(0, part, part)
            stage(v_t, 4, 0, 0)
            low_part(3, 1)
            stage(v_t, 5, 1, 1)
            dve.wait_ge(lr_split, 1)
            dve.tensor_tensor(w_lr[:, :, RANK:2 * RANK], lr_raw[:, :, :], w_lr[:, :, 0:RANK].bitcast(F32),
                              ALU.subtract).then_inc(lr_split, 1)

            def pair(i, last):
                plan = plan_projection()
                dsts = [None, stage_q, stage_k, v_t]
                for step in range(STEPS):
                    if step < 16:
                        keys = (step % 8 + 1) * P
                        s = surv[:, step % 2, 0:keys]
                        dve.wait_ge(sig_done, 16 * i + step + 2)
                        dve.tensor_tensor_scan(s[:, ::-1], s[:, ::-1], s[:, ::-1], 1.0, ALU.mult, ALU.bypass)\
                            .then_inc(scan_done, 1)
                        dve.wait_ge(scan_done, 16 * i + step + 1)
                        dve.tensor_tensor(beta[:, step % 2, 0:keys], beta[:, step % 2, 0:keys],
                                          surv[:, step % 2, 1:keys + 1], ALU.mult).then_inc(w_ready, 1)
                    for n, r in enumerate(ROUNDS):
                        if r[0] == "v" and r[1] == step:
                            dve.wait_ge(tr_act, RPP * i + R0 + n + 1)
                            vb = slice(4 * r[2], 4 * r[2] + 4)
                            dve.tensor_tensor(v_st[:, :, vb, HD:P],
                                              tr[n % 2][:, :].rearrange("p (b e d) -> p e b d", d=HD, e=2),
                                              v_st[:, :, vb, 0:HD].bitcast(F32), ALU.subtract).then_inc(tr_free, 1)
                    if step in SECOND_STEPS:
                        part = SECOND_STEPS.index(step)
                        stack(1, part, 6 * i + 3 + part)
                    if step in STACK_STEPS and not last:
                        part = STACK_STEPS.index(step)
                        stack(0, part, 6 * i + 6 + part)
                    for j, h, k, p in plan[step]:
                        if k < KT - 1 or p < 2:
                            continue
                        c = 8 * i + 6 + 2 * j + h
                        if h == 0:
                            low_part(4 * i + 4 + j, j % 2)
                        if j == 0:
                            dve.wait_ge(proj_act, c + 1)
                            dve.tensor_tensor(z_silu[:, HALF * h:HALF * h + HALF], pj[h][:, :], z_sig[:, :],
                                              ALU.mult).then_inc(proj_free, 1)
                        else:
                            stage(dsts[j], c, h, h)
                    if step >= 3 and step % 2:
                        gg = (step - 3) // 2
                        e, g = gg // 4, gg % 4
                        own = slice(HD * e, HD * e + HD)
                        low = o_low[own, gg % 2, :]
                        dve.wait_ge(o_copied, 8 * i + gg + 1)
                        dve.tensor_tensor(low, ob[gg % 2][0:HD, 0:256], low, ALU.add).then_inc(o_free, 1)
                        dve.wait_ge(o_free, 8 * i + gg + 3)
                        dve.wait_ge(proj_free, 8 * i + 7 + g // 2)
                        dve.tensor_tensor(G[own, bass.ds(i, 1), 256 * g:256 * g + 256].rearrange("p a c -> p (a c)"),
                                          low, z_silu[own, 256 * g:256 * g + 256], ALU.mult).then_inc(g_done, 1)
                    for n, r in enumerate(ROUNDS):
                        if r[0] == "w" and r[1] == step:
                            unit, b0, nb = r[2:]
                            g = unit % 8 // 2
                            qs = slice(P * (unit % 2), P * (unit % 2) + P)
                            dve.wait_ge(tr_act, RPP * i + R0 + n + 1)
                            dve.tensor_tensor(wt_lo[g % 2][:, b0:b0 + nb, qs],
                                              tr[n % 2][:, 0:P * nb].rearrange("p (b q) -> p b q", q=P),
                                              wt_hi[g % 2][:, b0:b0 + nb, qs].bitcast(F32),
                                              ALU.subtract).then_inc(tr_free, 1)

            with dve.Fori(0, PAIRS - 1) as i:
                pair(i, False)
            pair(PAIRS - 1, True)

            for h in range(2):
                dve.wait_ge(proj_act, BANK_LR + h + 1)
                dve.tensor_copy(lr_t[:, HALF * h + 256:HALF * h + HALF], pj[h][0:2 * RANK, 256:HALF])\
                    .then_inc(proj_free, 1)

            def body_evacuate(hp, j, h):
                n = body_tile(hp, j)
                kind, m = BODY[hp][j]
                c = bank_no(n) + h
                if kind == "z":
                    dve.wait_ge(proj_act, c + 1)
                    dve.tensor_tensor(gz[:, m % 2, HALF * h:HALF * h + HALF], pj[h][:, :], gz_sig[:, :],
                                      ALU.mult).then_inc(proj_free, 1)
                elif kind == "v":
                    stage(v_t, c, h, h)
                else:
                    stage(stage_q if kind == "q" else stage_k, c, h, h)
                if h == 0:
                    low_part(n + 1, (n + 1) % 2)

            def copy_round(n, act_no, dst):
                dve.wait_ge(tr_act, act_no + 1)
                dve.tensor_copy(dst, tr[n % 2][:, 256:HALF].rearrange("p (b d) -> p b d", d=P)).then_inc(tr_free, 1)

            def split_g(k):
                dve.wait_ge(gs_hi, k + 1)
                dve.tensor_tensor(g_lo[:, G_SLOT[k], :], G[:, k, :], g_hi[:, G_SLOT[k], :].bitcast(F32),
                                  ALU.subtract).then_inc(gs_lo, 1)

            t1, t2 = t12[:, 0, :], t12[:, 1, :]
            by_chunk = t1.rearrange("p (c s) -> p c s", s=CH)
            for hp in range(2):
                q0, s0, d0, r0 = Q_BODY * hp, 5 * hp, 7 * hp, R3 + R_BODY * hp
                a0 = R3 + 6 * hp
                bias = cols[:, 24 + hp:25 + hp]
                for ev in gla_events(hp):
                    kind = ev if isinstance(ev, str) else ev[0]
                    if kind == "alpha":
                        for h in range(2):
                            dve.wait_ge(q4_act, 6 * hp + h + 1)
                            dve.tensor_scalar(t2[:, HALF * h:HALF * h + HALF], ring4[(q0 + h) % 4], bias, 0.0,
                                              ALU.add, ALU.min).then_inc(q4_free, 1)
                    elif kind == "log1":
                        dve.wait_ge(q4_free, q0 + 2)
                        dve.wait_ge(act_step, s0 + 2)
                        dve.tensor_tensor(t2, t2, t1, ALU.subtract).then_inc(dve_step, 1)
                        dve.wait_ge(dve_step, d0 + 1)
                        dve.wait_ge(const_done, 13)
                        dve.tensor_tensor_scan(t1, reset[:, :], t2, 0.0, ALU.mult, ALU.add).then_inc(dve_step, 1)
                    elif kind == "log2":
                        dve.wait_ge(act_step, s0 + 3)
                        dve.scalar_tensor_tensor(out=q_dec[:, :], in0=stage_q[:, :], scalar=HD ** -0.5, in1=t2,
                                                 op0=ALU.mult, op1=ALU.mult).then_inc(dve_step, 1)
                        dve.tensor_copy(stats[:, 48:48 + NCH - 1], t2[:, CH - 1:SEQ - CH:CH]).then_inc(dve_step, 1)
                        dve.wait_ge(act_step, s0 + 4)
                        dve.tensor_tensor(k_inv[:, :], stage_k[:, :], t3[:, :], ALU.mult).then_inc(dve_step, 1)
                        dve.wait_ge(dve_step, d0 + 4)
                        dve.tensor_tensor(t2.rearrange("p (c s) -> p c s", s=CH),
                                          by_chunk[:, :, CH - 1:CH].to_broadcast([P, NCH, CH]), by_chunk,
                                          ALU.subtract).then_inc(dve_step, 1)
                    elif kind == "end":
                        dve.wait_ge(act_step, s0 + 5)
                        dve.wait_ge(dve_step, d0 + 6)
                        dve.tensor_tensor(t3[:, :], stage_k[:, :], t2, ALU.mult).then_inc(dve_step, 1)
                    elif kind == "ev":
                        body_evacuate(hp, ev[1], ev[2])
                    elif kind in ("v0", "v1"):
                        j = int(kind[1])
                        for r in range(2):
                            copy_round(r0 + TURN[hp][kind] + r, a0 + TURN[hp][kind] + r,
                                       v_nat[:, 4 * r + 2:4 * r + 4, DV * j:DV * j + DV])
                    elif kind in ("k0", "k1"):
                        r = int(kind[1])
                        copy_round(r0 + TURN[hp][kind], a0 + TURN[hp][kind], k_end[:, 4 * r + 2:4 * r + 4, :])
                    elif kind.startswith("kv"):
                        c = int(kind[2:])
                        q = q0 + 2 + c
                        dec = stats[:, 48 + c:49 + c]
                        dve.wait_ge(q4_ready, q + 1)
                        if c:
                            dve.wait_ge(q4_free, q)
                        for e in range(2):
                            own = slice(HD * e, HD * e + HD)
                            ins = dve.scalar_tensor_tensor(out=state[own, c + 1, :], in0=state[own, c, :],
                                                           scalar=dec[own, :],
                                                           in1=ring4[q % 4][own, DV * e:DV * e + DV],
                                                           op0=ALU.mult, op1=ALU.add)
                        ins.then_inc(q4_free, 1)
                    elif kind.startswith("sc"):
                        r = int(kind[2:])
                        q, e, b0 = q0 + 2 + NCH - 1 + r, r % 2, 4 * (r // 2)
                        dve.wait_ge(q4_ready, q + 1)
                        dve.copy_predicated(sT[:, e, b0:b0 + 4, :], mask4[:, :, :].bitcast(I32),
                                            ring4[q % 4].rearrange("p (b q) -> p b q", q=P)).then_inc(q4_free, 1)
                    elif kind in ("o0", "o1", "o2", "o3"):
                        r = int(kind[1])
                        q, e, b0 = q0 + 2 + NCH - 1 + 4 + r, r % 2, 4 * (r // 2)
                        dve.wait_ge(q4_act, 6 * hp + 2 + r + 1)
                        dve.tensor_copy(o_nat[:, e, b0:b0 + 4, :], ring4[q % 4].rearrange("p (b q) -> p b q", q=P))\
                            .then_inc(q4_free, 1)
                    elif kind == "norm":
                        dve.wait_ge(sq_done, 2 * ST + hp + 1)
                        dve.reciprocal(stats[:, 32:48], stats[:, 32:48]).then_inc(rstd_ready, 1)
                        dve.wait_ge(rstd_ready, ST + 2 * hp + 1)
                        o_flat = o_nat.rearrange("p e b q -> p (e b) q")
                        dve.wait_ge(q4_free, Q_BODY * (hp + 1))
                        dve.tensor_tensor(o_flat, o_flat,
                                          stats[:, 32:48].rearrange("p (a b) -> p a b", b=1).to_broadcast([P, 16, P]),
                                          ALU.mult).then_inc(rstd_ready, 1)
                    elif kind == "gs":
                        split_g(ev[1])
                    elif kind == "gate":
                        low_part(N4 + 1, (N4 + 1) % 2)
                    elif kind.startswith("out"):
                        r = int(kind[3])
                        n, e, half = r0 + 6 + r, r // 2, r % 2
                        hs = slice(HALF * half, HALF * half + HALF)
                        dve.wait_ge(proj_free, bank_no(body_tile(hp, 3)) + 2)
                        dve.wait_ge(tr_ready, n + 1)
                        dve.scalar_tensor_tensor(out=G[:, 4 + 2 * hp + e, hs], in0=tr[n % 2][:, :],
                                                 scalar=cols[:, 26:27], in1=gz[:, e, hs], op0=ALU.mult,
                                                 op1=ALU.mult).then_inc(tr_free, 1)

            dve.wait_ge(tr_free, R3 + 2 * R_BODY)
            for k in range(4, 8):
                split_g(k)

            def split_m0(part):
                ks = slice(0, KT - 1) if part == 0 else slice(KT - 1, KT)
                dve.wait_ge(m0_hi, part + 1)
                dve.tensor_tensor(w_lo[:, N5 % 2, ks, :], mT[:, ks, 0:P], w_hi[:, N5 % 2, ks, :].bitcast(F32),
                                  ALU.subtract).then_inc(m0_lo, 1)

            def wout_low(c):
                e, kk = c // 4, 2 * (c % 4)
                dve.wait_ge(wout_h, c + 1)
                dve.tensor_tensor(wout_lo[e][:, kk:kk + 2, :], wout_raw[:, kk:kk + 2, HALF * e:HALF * e + HALF],
                                  wout_hi[e][:, kk:kk + 2, :].bitcast(F32), ALU.subtract).then_inc(wout_l, 1)

            def merge(jj, last):
                for u in range(2):
                    n = 6 * jj + N4 + 3 * u
                    end = last and u == 1
                    low_part(n + 2, (N4 + 3 * u + 2) % 2)
                    if end:
                        split_m0(0)
                    else:
                        low_part(n + 3, (N4 + 3 * u + 3) % 2)
                    dve.wait_ge(gate_free, 8 * jj + 4 * u + 4 + 2)
                    for h in range(2):
                        for br in range(2):
                            c = 8 * jj + 4 * u + 2 * h + br
                            dve.wait_ge(y_ready, c + 2)
                            dve.tensor_tensor(y_g[h][:, br, :], ring4[2 * h + br], gate[:, br, HALF * h:HALF * h + HALF],
                                              ALU.mult).then_inc(y_free, 1)
                        dve.wait_ge(y_free, 8 * jj + 4 * u + 2 * h + 2 + 4)
                        dve.tensor_tensor(
                            mT[:, bass.ds(2 * jj + u, 1), HALF * h:HALF * h + HALF].rearrange("p a c -> p (a c)"),
                            y_g[h][:, 0, :], y_g[h][:, 1, :], ALU.add).then_inc(m_ready, 1)
                        if end and h == 0:
                            wout_low(0)
                            wout_low(1)
                    if not end:
                        low_part(n + 4, (N4 + 3 * u + 4) % 2)

            with dve.Fori(0, KT // 2 - 1) as jj:
                merge(jj, False)
            merge(KT // 2 - 1, True)

            def split_m(t):
                slot = (N5 + t) % 2
                dve.wait_ge(hi_done, N5 + t)
                dve.tensor_tensor(w_lo[:, slot, :, :], mT[:, :, P * t:P * t + P], w_hi[:, slot, :, :].bitcast(F32),
                                  ALU.subtract).then_inc(lo_done, 1)

            wout_low(2)
            split_m0(1)
            for c in range(3, KT):
                wout_low(c)
            dve.wait_ge(fin_bc, 1)
            for t in range(ST):
                if t + 1 < ST:
                    split_m(t + 1)
                dve.wait_ge(xr_loaded[t % 2], 16 * (t // 2 + 1))
                for e in range(2):
                    c = 2 * t + e
                    es = slice(HALF * e, HALF * e + HALF)
                    dve.wait_ge(o5_ready, c + 1)
                    dve.tensor_tensor(y_row[:, t % 2, es], ring4[c % 4], x_res[:, t % 2, es], ALU.add)\
                        .then_inc(o5_free, 1)
                dve.wait_ge(ss5, 2 * t + 2)
                dve.reciprocal(stats[:, 52 + t % 2:53 + t % 2], stats[:, 50 + t % 2:51 + t % 2]).then_inc(rstd5, 1)
                dve.wait_ge(rstd5, t + 1)
                if t >= 2:
                    dve.wait_ge(stored[t % 2], 32 * (t // 2))
                for e in range(2):
                    es = slice(HALF * e, HALF * e + HALF)
                    dve.scalar_tensor_tensor(out=y_out[:, t % 2, es], in0=y_row[:, t % 2, es],
                                             scalar=stats[:, 52 + t % 2:53 + t % 2], in1=g_fin[:, es],
                                             op0=ALU.mult, op1=ALU.mult).then_inc(y_done, 1)


_INS = ["x", "g_pre", "w_in", "b_gate", "w_alpha_up", "b_alpha_up", "g_gla_norm",
        "w_o_sb", "w_o_gla", "w_out", "g_final"]


def kernel(**inputs):
    import numpy as np
    import concourse.bacc as bacc
    from concourse.bass_utils import run_bass_kernel_spmd

    nc = bacc.Bacc("TRN2", target_bir_lowering=False, num_devices=1)
    arrays, args = {}, []
    for name in _INS:
        a = np.ascontiguousarray(inputs[name])
        arrays[f"in_{name}"] = a
        args.append(nc.dram_tensor(f"in_{name}", a.shape, mybir.dt.from_np(a.dtype), kind="ExternalInput").ap())
    args.append(nc.dram_tensor("out_y", (1, SEQ, D), F32, kind="ExternalOutput").ap())
    stickbreak_gla_hybrid(nc, *args)
    r = run_bass_kernel_spmd(nc, [arrays], core_ids=[0])
    return r.results[0]["out_y"]
```
